# Optimizing a Trainium2 kernel written in Bass

```python
import math
import jax, jax.numpy as jnp
from jax import lax
import numpy as np

D_MODEL = 1024
BATCH = 1
SEQ = 1024
DEPTH = 2

D_MIX = D_MODEL
DIFF_HEADS = 4
DIFF_WIDTH = D_MIX // 2
DIFF_V_DIM = DIFF_WIDTH // DIFF_HEADS
DIFF_QK_DIM = DIFF_V_DIM // 2
MLA_HEADS = 4
MLA_WIDTH = D_MIX // 4
MLA_V_DIM = MLA_WIDTH // MLA_HEADS
MLA_NOPE_DIM = 64
MLA_ROPE_DIM = 32
MLA_Q_RANK = 192
MLA_KV_RANK = 128
ROPE_BASE = 10000.0
POOL_WIDTH = D_MIX - DIFF_WIDTH - MLA_WIDTH
POOL_GROUPS = 4
POOL_GROUP_DIM = POOL_WIDTH // POOL_GROUPS
POOL_WINDOWS = (2, 4, 8, 16)
IN_WIDTHS = (DIFF_HEADS * 2 * DIFF_QK_DIM, DIFF_HEADS * 2 * DIFF_QK_DIM, DIFF_WIDTH,
             MLA_Q_RANK, MLA_KV_RANK, MLA_ROPE_DIM, POOL_WIDTH)
D_IN = sum(IN_WIDTHS)
IN_SPLITS = tuple(sum(IN_WIDTHS[:i + 1]) for i in range(len(IN_WIDTHS) - 1))
N_GROUPS = 4
EXPERTS_PER_GROUP = 8
N_EXPERTS = N_GROUPS * EXPERTS_PER_GROUP
TOP_K = 2
D_FF_EXPERT = 256
ROUTE_BLOCK = 256
Q_BLOCK = 128
RMS_EPS = 1e-6

kernel_name = 'hybrid_diffattn_mla_pool_hmoe_encoder'

def _rms_norm(x, g):
    xf = x.astype(jnp.float32)
    y = xf * lax.rsqrt(jnp.mean(xf * xf, axis=-1, keepdims=True) + RMS_EPS)
    return (y * g.astype(jnp.float32)).astype(x.dtype)

def _to_blocks(x):
    b, s = x.shape[0], x.shape[1]
    return jnp.moveaxis(x.reshape((b, s // Q_BLOCK, Q_BLOCK) + x.shape[2:]), 1, 0)

def _from_blocks(y):
    nb, b, qb = y.shape[0], y.shape[1], y.shape[2]
    return jnp.moveaxis(y, 0, 1).reshape((b, nb * qb) + y.shape[3:])

def _alibi_slopes(n_heads):
    return 2.0 ** (-8.0 * jnp.arange(1, n_heads + 1, dtype=jnp.float32) / n_heads)

def _diff_attention(q1, q2, k1, k2, v, lam):
    s = q1.shape[1]
    scale = q1.shape[-1] ** -0.5
    slopes = _alibi_slopes(q1.shape[2])
    k_pos = jnp.arange(s, dtype=jnp.int32)
    q_pos = k_pos.reshape(s // Q_BLOCK, Q_BLOCK)

    def block(args):
        q1b, q2b, qp = args
        dist = jnp.abs(qp[:, None] - k_pos[None, :]).astype(jnp.float32)
        bias = -slopes[:, None, None] * dist[None]
        s1 = jnp.einsum('bqhd,bkhd->bhqk', q1b, k1, preferred_element_type=jnp.float32) * scale + bias
        s2 = jnp.einsum('bqhd,bkhd->bhqk', q2b, k2, preferred_element_type=jnp.float32) * scale + bias
        a = jax.nn.softmax(s1, axis=-1) - lam * jax.nn.softmax(s2, axis=-1)
        return jnp.einsum('bhqk,bkhe->bqhe', a.astype(v.dtype), v)

    return _from_blocks(lax.map(block, (_to_blocks(q1), _to_blocks(q2), q_pos)))

def _rope_tables(s):
    inv = 1.0 / (ROPE_BASE ** (jnp.arange(0, MLA_ROPE_DIM, 2, dtype=jnp.float32) / MLA_ROPE_DIM))
    ang = jnp.arange(s, dtype=jnp.float32)[:, None] * inv[None, :]
    return jnp.cos(ang), jnp.sin(ang)

def _rotate(x, cos, sin):
    half = x.shape[-1] // 2
    x1 = x[..., :half].astype(jnp.float32)
    x2 = x[..., half:].astype(jnp.float32)
    return jnp.concatenate([x1 * cos - x2 * sin, x2 * cos + x1 * sin], axis=-1).astype(x.dtype)

def _mla_attention(q_nope, q_rope, k_nope, k_rope, v):
    scale = (q_nope.shape[-1] + q_rope.shape[-1]) ** -0.5

    def block(args):
        qn, qr = args
        sc = (jnp.einsum('bqhd,bkhd->bhqk', qn, k_nope, preferred_element_type=jnp.float32)
              + jnp.einsum('bqhr,bkr->bhqk', qr, k_rope, preferred_element_type=jnp.float32)) * scale
        p = jax.nn.softmax(sc, axis=-1)
        return jnp.einsum('bhqk,bkhe->bqhe', p.astype(v.dtype), v)

    return _from_blocks(lax.map(block, (_to_blocks(q_nope), _to_blocks(q_rope))))

def _multi_scale_pool(u, w, scale):
    b, s, c = u.shape
    uf = u.astype(jnp.float32).reshape(b, s, POOL_GROUPS, POOL_GROUP_DIM)
    cs = jnp.concatenate([jnp.zeros((b, 1, POOL_GROUPS, POOL_GROUP_DIM), jnp.float32),
                          jnp.cumsum(uf, axis=1)], axis=1)
    t = jnp.arange(s, dtype=jnp.int32)
    outs = []
    for g, win in enumerate(POOL_WINDOWS):
        lo = jnp.clip(t - win // 2, 0, s - 1)
        hi = jnp.clip(t + win // 2 - 1, 0, s - 1)
        csg = cs[:, :, g]
        win_sum = jnp.take(csg, hi + 1, axis=1) - jnp.take(csg, lo, axis=1)
        cnt = (hi - lo + 1).astype(jnp.float32)
        outs.append(win_sum / cnt[None, :, None] - uf[:, :, g])
    pooled = jnp.stack(outs, axis=2).astype(u.dtype)
    mixed = jnp.einsum('bsgc,gcd->bsgd', pooled, w)
    return mixed.reshape(b, s, c) * scale

def _hier_moe(h, wg, bg, we, be, w_gate, w_up, w_down):
    b, s, d = h.shape
    t = b * s
    hf = h.reshape(t, d)
    g_prob = jax.nn.softmax((hf @ wg).astype(jnp.float32) + bg.astype(jnp.float32), axis=-1)
    g_top, g_idx = lax.top_k(g_prob, 1)
    e_logits = ((hf @ we).astype(jnp.float32) + be.astype(jnp.float32)).reshape(t, N_GROUPS, EXPERTS_PER_GROUP)
    e_sel = e_logits[jnp.arange(t), g_idx[:, 0]]
    e_top, e_idx = lax.top_k(jax.nn.softmax(e_sel, axis=-1), TOP_K)
    gate = g_top * e_top / jnp.sum(e_top, axis=-1, keepdims=True)
    expert_id = (g_idx * EXPERTS_PER_GROUP + e_idx).reshape(-1).astype(jnp.int32)
    token_id = jnp.repeat(jnp.arange(t, dtype=jnp.int32), TOP_K)
    weight = gate.reshape(-1)
    n_assign = t * TOP_K
    n_blocks = n_assign // ROUTE_BLOCK + N_EXPERTS
    cap = n_blocks * ROUTE_BLOCK
    order = jnp.argsort(expert_id)
    sorted_eid = expert_id[order]
    counts = jnp.bincount(expert_id, length=N_EXPERTS)
    starts = jnp.cumsum(counts) - counts
    padded = (counts + ROUTE_BLOCK - 1) // ROUTE_BLOCK * ROUTE_BLOCK
    padded_ends = jnp.cumsum(padded)
    padded_starts = padded_ends - padded
    dest = padded_starts[sorted_eid] + jnp.arange(n_assign, dtype=jnp.int32) - starts[sorted_eid]
    slot_tok = jnp.full((cap,), t, jnp.int32).at[dest].set(token_id[order])
    slot_w = jnp.zeros((cap,), jnp.float32).at[dest].set(weight[order])
    block_start = jnp.arange(n_blocks, dtype=jnp.int32) * ROUTE_BLOCK
    block_eid = jnp.minimum(jnp.sum(block_start[:, None] >= padded_ends[None, :], axis=1), N_EXPERTS - 1)
    xs = jnp.concatenate([hf, jnp.zeros((1, d), hf.dtype)], axis=0)[slot_tok].reshape(n_blocks, ROUTE_BLOCK, d)

    def expert_block(args):
        xb, e = args
        return (jax.nn.silu(xb @ w_gate[e]) * (xb @ w_up[e])) @ w_down[e]

    ys = lax.map(expert_block, (xs, block_eid)).reshape(cap, d)
    y = jnp.zeros((t + 1, d), jnp.float32).at[slot_tok].add(ys.astype(jnp.float32) * slot_w[:, None])
    return y[:t].astype(h.dtype).reshape(b, s, d)

def setup_inputs(seed: int = 0) -> dict:
    key = jax.random.key(seed)
    ks = jax.random.split(key, 26)
    f32 = jnp.float32
    L = DEPTH

    def nrm(k, shape, fan_in):
        return jax.random.normal(k, shape, f32) * (fan_in ** -0.5)

    def gain(k, shape):
        return 1.0 + 0.02 * jax.random.normal(k, shape, f32)

    return {
        'x': jax.random.normal(ks[0], (BATCH, SEQ, D_MODEL), f32),
        'norm1_g': gain(ks[1], (L, D_MODEL)),
        'w_in': nrm(ks[2], (L, D_MODEL, D_IN), D_MODEL),
        'diff_q_norm_g': gain(ks[3], (L, DIFF_QK_DIM)),
        'diff_k_norm_g': gain(ks[4], (L, DIFF_QK_DIM)),
        'diff_lambda': 0.1 * jax.random.normal(ks[5], (L, 4, DIFF_QK_DIM), f32),
        'diff_sub_norm_g': gain(ks[6], (L, DIFF_V_DIM)),
        'mla_q_lat_norm_g': gain(ks[7], (L, MLA_Q_RANK)),
        'mla_kv_lat_norm_g': gain(ks[8], (L, MLA_KV_RANK)),
        'mla_w_uq': nrm(ks[9], (L, MLA_Q_RANK, MLA_HEADS * (MLA_NOPE_DIM + MLA_ROPE_DIM)), MLA_Q_RANK),
        'mla_w_ukv': nrm(ks[10], (L, MLA_KV_RANK, MLA_HEADS * (MLA_NOPE_DIM + MLA_V_DIM)), MLA_KV_RANK),
        'mla_q_nope_norm_g': gain(ks[11], (L, MLA_NOPE_DIM)),
        'mla_q_rope_norm_g': gain(ks[12], (L, MLA_ROPE_DIM)),
        'mla_k_nope_norm_g': gain(ks[13], (L, MLA_NOPE_DIM)),
        'mla_k_rope_norm_g': gain(ks[14], (L, MLA_ROPE_DIM)),
        'pool_w': nrm(ks[15], (L, POOL_GROUPS, POOL_GROUP_DIM, POOL_GROUP_DIM), POOL_GROUP_DIM),
        'pool_scale': gain(ks[16], (L, POOL_WIDTH)),
        'w_out': nrm(ks[17], (L, D_MIX, D_MODEL), D_MIX),
        'norm2_g': gain(ks[18], (L, D_MODEL)),
        'router_group_w': nrm(ks[19], (L, D_MODEL, N_GROUPS), D_MODEL),
        'router_group_b': 0.01 * jax.random.normal(ks[20], (L, N_GROUPS), f32),
        'router_expert_w': nrm(ks[21], (L, D_MODEL, N_EXPERTS), D_MODEL),
        'router_expert_b': 0.01 * jax.random.normal(ks[22], (L, N_EXPERTS), f32),
        'expert_w_gate': nrm(ks[23], (L, N_EXPERTS, D_MODEL, D_FF_EXPERT), D_MODEL),
        'expert_w_up': nrm(ks[24], (L, N_EXPERTS, D_MODEL, D_FF_EXPERT), D_MODEL),
        'expert_w_down': nrm(ks[25], (L, N_EXPERTS, D_FF_EXPERT, D_MODEL), D_FF_EXPERT),
    }

def reference(x, norm1_g, w_in, diff_q_norm_g, diff_k_norm_g, diff_lambda, diff_sub_norm_g,
              mla_q_lat_norm_g, mla_kv_lat_norm_g, mla_w_uq, mla_w_ukv,
              mla_q_nope_norm_g, mla_q_rope_norm_g, mla_k_nope_norm_g, mla_k_rope_norm_g,
              pool_w, pool_scale, w_out, norm2_g,
              router_group_w, router_group_b, router_expert_w, router_expert_b,
              expert_w_gate, expert_w_up, expert_w_down):
    b, s, _ = x.shape
    cos, sin = _rope_tables(s)
    for l in range(DEPTH):
        lam_init = 0.8 - 0.6 * math.exp(-0.3 * l)
        h = _rms_norm(x, norm1_g[l])
        proj = h @ w_in[l]
        dq, dk, dv, cq, ckv, kr, pu = jnp.split(proj, IN_SPLITS, axis=-1)

        dq = _rms_norm(dq.reshape(b, s, DIFF_HEADS, 2, DIFF_QK_DIM), diff_q_norm_g[l])
        dk = _rms_norm(dk.reshape(b, s, DIFF_HEADS, 2, DIFF_QK_DIM), diff_k_norm_g[l])
        dv = dv.reshape(b, s, DIFF_HEADS, DIFF_V_DIM)
        lv = diff_lambda[l].astype(jnp.float32)
        lam = jnp.exp(jnp.sum(lv[0] * lv[1])) - jnp.exp(jnp.sum(lv[2] * lv[3])) + lam_init
        o_diff = _diff_attention(dq[..., 0, :], dq[..., 1, :], dk[..., 0, :], dk[..., 1, :], dv, lam)
        o_diff = (_rms_norm(o_diff, diff_sub_norm_g[l]) * (1.0 - lam_init)).reshape(b, s, DIFF_WIDTH)

        q = (_rms_norm(cq, mla_q_lat_norm_g[l]) @ mla_w_uq[l]).reshape(b, s, MLA_HEADS, MLA_NOPE_DIM + MLA_ROPE_DIM)
        kv = (_rms_norm(ckv, mla_kv_lat_norm_g[l]) @ mla_w_ukv[l]).reshape(b, s, MLA_HEADS, MLA_NOPE_DIM + MLA_V_DIM)
        q_nope = _rms_norm(q[..., :MLA_NOPE_DIM], mla_q_nope_norm_g[l])
        q_rope = _rotate(_rms_norm(q[..., MLA_NOPE_DIM:], mla_q_rope_norm_g[l]),
                         cos[None, :, None, :], sin[None, :, None, :])
        k_nope = _rms_norm(kv[..., :MLA_NOPE_DIM], mla_k_nope_norm_g[l])
        k_rope = _rotate(_rms_norm(kr, mla_k_rope_norm_g[l]), cos[None], sin[None])
        o_mla = _mla_attention(q_nope, q_rope, k_nope, k_rope, kv[..., MLA_NOPE_DIM:]).reshape(b, s, MLA_WIDTH)

        o_pool = _multi_scale_pool(pu, pool_w[l], pool_scale[l])

        x = x + jnp.concatenate([o_diff, o_mla, o_pool], axis=-1) @ w_out[l]

        x = x + _hier_moe(_rms_norm(x, norm2_g[l]), router_group_w[l], router_group_b[l],
                          router_expert_w[l], router_expert_b[l],
                          expert_w_gate[l], expert_w_up[l], expert_w_down[l])
    return x


_drawn_inputs = setup_inputs


def setup_inputs(seed=0):
    import zlib

    import numpy as np

    out = dict(_drawn_inputs(seed))
    spreads = {}
    factors = {'mla_q_lat_norm_g': 8.0,
     'mla_kv_lat_norm_g': 6.142,
     'mla_q_nope_norm_g': 8.0,
     'mla_q_rope_norm_g': 8.0,
     'mla_k_nope_norm_g': 8.0,
     'mla_k_rope_norm_g': 8.0,
     'router_group_b': 4.408,
     'router_expert_b': 3.079}
    for name, (base, spread) in spreads.items():
        noise = np.random.default_rng([zlib.crc32(name.encode()), seed]).standard_normal(out[name].shape)
        drawn = base * np.exp(spread * noise) if base else spread * noise
        out[name] = __import__('jax').numpy.asarray(drawn.astype(out[name].dtype))
    for name, factor in factors.items():
        out[name] = (out[name] * factor).astype(out[name].dtype)
    return out
```

```python
import math
from collections import namedtuple
from contextlib import ExitStack, contextmanager

import concourse.bass as bass
from concourse import mybir

F32 = mybir.dt.float32
F16 = mybir.dt.float16
BF16 = mybir.dt.bfloat16
I32 = mybir.dt.int32
U32 = mybir.dt.uint32
ALU = mybir.AluOpType
ACT = mybir.ActivationFunctionType
AX = mybir.AxisListType

P = 128
SEQ = 1024
D = 1024
DEPTH = 2
NT = SEQ // P
KD = D // P
HALF = 512
DH = 4
DV = 128
DQ = 64
MH = 4
NOPE, ROPE, MV = 64, 32, 64
MQ = NOPE + ROPE
QR, KVR = 192, 128
PW = 256
WINDOWS = (2, 4, 8, 16)
PAD = 8
D_IN = 2144
O_LAT = 1024
O_KR = O_LAT + QR + KVR
O_PU = O_KR + ROPE
PJ = O_PU + PW
CHUNKS = ((0, 512), (512, 512), (1024, 512), (1536, 352), (1888, 256))
NG, EPG = 4, 8
NE = NG * EPG
FF = 256
CAP = 96
OVER = -(-SEQ // CAP) - 1
SLOT = 2 * KD * FF + 2 * D
EPS = 1e-6
NLOG = NG + NE
OOB = 4096
NSTAT = 19

C_DQG, C_DKG, C_SUB, C_QL, C_KVL, C_MQG, C_MKG, C_PS = 0, 1, 2, 3, 5, 6, 7, 8
C_RGQ, C_RSQ, C_RGK, C_RSK = 10, 42, 74, 106
C_RB = 138
C_LAM = C_RB + NLOG
C_LI = C_LAM + 4 * DQ
N_SM = C_LI + 2
K_ID, K_COS, K_SIN, K_INV, K_INV2, K_I8, K_TILE, K_P, K_TRI, K_NH = 0, 128, 384, 640, 659, 671, 679, 687, 688, 816
N_K = K_NH + 24


class Count:

    def __init__(self, sem, per_layer, unit=1):
        self.sem, self.per_layer, self.unit = sem, per_layer, unit
        self.k = 0
        self.layer = self.step = None
        self.per_step = 0

    def value(self, k):
        v = self.layer * (self.per_layer * self.unit) if self.layer is not None else 0
        if self.step is not None and self.per_step:
            v = v + self.step * (self.per_step * self.unit)
        return v + k * self.unit

    def next(self, n=1):
        self.k += n
        return self.value(self.k)

    def last(self):
        return self.value(self.k)


class Counts:

    def __init__(self, name):
        self.name, self.all = name, {}
        self.table, self.loops = USES.get(name, {}), LOOP_USES.get(name, {})
        self.seen, self.seen_loops = {}, {}

    def on(self, sem, key, unit=1):
        c = self.all[key] = Count(sem, self.table.get(key, 0), unit)
        return c

    def enter_layer(self, layer):
        for c in self.all.values():
            c.layer, c.k = layer, 0

    def leave_layer(self):
        self.seen = {key: c.k for key, c in self.all.items() if c.k}
        if self.seen != self.table or self.seen_loops != self.loops:
            raise ValueError((self.name, self.seen, self.seen_loops))

    @contextmanager
    def loop(self, eng, key, first, end, by=1):
        per_step = self.loops.get(key, {})
        with eng.Fori(first, end) as step:
            start = {}
            for k, c in self.all.items():
                c.per_step = per_step.get(k, 0)
                c.step, start[k] = step, c.k
                c.k -= c.per_step * first
            yield step
        self.seen_loops[key] = {}
        for k, c in self.all.items():
            used = c.k + c.per_step * first - start[k]
            if used:
                self.seen_loops[key][k] = used
            c.k = start[k] + used * (end - first)
            c.step, c.per_step = None, 0


USES = {'act': {'phase': 20,
         'ta': 153,
         'mine': 153,
         'x': 16,
         'pf': 40,
         'qst': 8,
         'biased': 64,
         'max': 32,
         'xup': 16,
         'rarg': 2,
         'lam': 1,
         'gf': 32,
         'dn': 32,
         's0': 16,
         's1': 16,
         'cxr': 16,
         'cxs0': 4,
         'cxs1': 4,
         'small': 1},
 'dve': {'phase': 20,
         'step': 398,
         'tb': 185,
         'mine': 185,
         'xsq': 16,
         'rstd': 40,
         'kept': 40,
         'gl': 2,
         'bl': 8,
         'lamx': 1,
         'sr': 96,
         'exp': 96,
         'pv': 64,
         'x': 16,
         'hst': 8,
         'iota': 1,
         'rex': 2,
         'rank': 1,
         'ids': 34,
         'silu': 32,
         'up': 32,
         'dn': 32,
         's0': 16,
         's1': 16,
         'cx0': 12,
         'cx1': 12,
         'cxr': 16,
         'small': 1,
         'xup': 16},
 'pe': {'phase': 20,
        'ta': 153,
        'tb': 185,
        'xn': 8,
        'kept': 40,
        'pjn': 8,
        'mln': 8,
        'win': 1,
        'ql': 8,
        'wo': 1,
        'biased': 64,
        'exp': 96,
        'mixed': 32,
        'od': 8,
        'om': 8,
        'pooled': 1,
        'hf': 8,
        'mask': 1,
        'oh': 34,
        'g0': 17,
        'g1': 17,
        'w0': 24,
        'w1': 24,
        'w2': 24,
        'w3': 24,
        'h': 32,
        'ya': 32,
        'yb': 32,
        'small': 1,
        'wr': 1,
        'wt': 4},
 'pool': {'phase': 20,
          'step': 13,
          'var': 40,
          'inv': 4,
          'ids': 34,
          'ya': 32,
          'yb': 32,
          's0': 16,
          's1': 16,
          'g0': 17,
          'g1': 17},
 'sp': {'phase': 20,
        'xn': 8,
        'sr': 96,
        'biased': 64,
        'xup': 16,
        'hf': 8,
        'xst': 8,
        'hst': 8,
        'pooled': 1,
        'dn': 32,
        'cxs0': 4,
        'cxs1': 4}}
LOOP_USES = {'act': {'p1': {'ta': 4, 'mine': 4, 'x': 1, 'pf': 5, 'qst': 1},
         'p2': {'ta': 11, 'mine': 11, 'biased': 8, 'max': 4, 'xup': 2},
         'p3': {'ta': 4, 'mine': 4, 'gf': 4, 'dn': 4, 's0': 2, 's1': 2},
         'p4': {'cxr': 4, 'cxs0': 1, 'cxs1': 1}},
 'dve': {'p1': {'step': 25, 'tb': 6, 'mine': 6, 'xsq': 1, 'rstd': 3, 'kept': 5},
         'p2': {'step': 15,
                'tb': 13,
                'mine': 13,
                'xsq': 1,
                'rstd': 2,
                'bl': 1,
                'sr': 12,
                'exp': 12,
                'pv': 8,
                'x': 1,
                'hst': 1,
                'xup': 2},
         'p3': {'step': 4, 'tb': 4, 'mine': 4, 'ids': 4, 'silu': 4, 'up': 4, 'dn': 4, 's0': 2, 's1': 2},
         'p4': {'cx0': 3, 'cx1': 3, 'cxr': 4}},
 'pe': {'p1': {'ta': 4, 'tb': 6, 'xn': 1, 'kept': 5, 'pjn': 1, 'mln': 1},
        'p2': {'ta': 11, 'tb': 13, 'ql': 1, 'biased': 8, 'exp': 12, 'mixed': 4, 'od': 1, 'om': 1, 'hf': 1},
        'p3': {'ta': 4,
               'tb': 4,
               'oh': 4,
               'g0': 2,
               'g1': 2,
               'w0': 3,
               'w1': 3,
               'w2': 3,
               'w3': 3,
               'h': 4,
               'ya': 4,
               'yb': 4}},
 'pool': {'p1': {'var': 3}, 'p2': {'var': 2}, 'p3': {'ids': 4, 'ya': 4, 'yb': 4, 's0': 2, 's1': 2, 'g0': 2, 'g1': 2}},
 'sp': {'p1': {'xn': 1},
        'p2': {'sr': 12, 'biased': 8, 'xup': 2, 'hf': 1, 'xst': 1, 'hst': 1},
        'p3': {'dn': 4},
        'p4': {'cxs0': 1, 'cxs1': 1}}}


def program(nc, x, w_in, w_uq, w_ukv, pool_w, w_out, w_router, w_gate, w_up, w_down,
            small, gain_rows, consts, alibi, inv_count, slots_iota, out):
    dram = lambda name, shape: nc.dram_tensor(name, shape, F32, kind="Internal").ap()
    q_dram = dram("q_dram", [NT, P, 2 * HALF])
    h_dram = dram("h_dram", [SEQ, D])
    y_dram = dram("y_dram", [2 * SEQ, D])
    xs = out[0]

    ctx = ExitStack()
    with ctx, nc.allow_low_precision(reason="whole numbers below 2**24 become indices"):
        sb = lambda name, shape, dt=F32: ctx.enter_context(nc.sbuf_tensor(name, shape, dt))
        sem = lambda name: ctx.enter_context(nc.semaphore(name))

        sm = sb("sm", [P, DEPTH, N_SM])
        cur = sb("cur", [P, N_SM])
        der = sb("der", [P, 16])
        cst = sb("cst", [P, N_K])
        grow = sb("grow", [P, D])
        put = sb("put", [P, 2, PAD + SEQ + PAD])
        tri = sb("tri", [P, P], BF16)
        ones = sb("ones", [P, P], BF16)
        logits = sb("logits", [P, NT, NLOG])
        gates = sb("gates", [P, 2, NT])
        nmax = sb("nmax", [P, 1], I32)
        st = sb("st", [P, 3, 24])
        pwd = sb("pwd", [P, 2, P])
        wreg = sb("wreg", [P, 3 * SLOT])
        qreg = sb("qreg", [P, 14336])
        WORK = 13060
        work = sb("work", [P, WORK])

        def flat(region, start, shape):
            n = math.prod(shape)
            assert start + n <= region.shape[1], (start, shape)
            a = region[:, start:start + n]
            if len(shape) == 2:
                a = a.rearrange("p (a b) -> p a b", b=shape[1])
            if len(shape) == 3:
                a = a.rearrange("p (a b c) -> p a b c", b=shape[1], c=shape[2])
            return a

        class Lay:
            def __init__(self, region, at=0):
                self.region, self.at = region, at

            def take(self, *shape):
                a = flat(self.region, self.at, shape)
                self.at += math.prod(shape)
                return a

        L = Lay(qreg)
        kT = L.take(DH, SEQ)
        kmT = L.take(MH, SEQ)
        V = L.take(NT, DH * DV)
        VM = L.take(NT, MH * MV)
        win = flat(wreg, 0, (KD, D_IN))
        L = Lay(work)
        xt1, xn1, junk1 = L.take(D), L.take(D), L.take(D)
        hT1 = L.take(KD, P)
        pj = L.take(PJ)
        sq = L.take(O_PU)
        mj = L.take(MH * MQ + MH * P)
        qc, kc = L.take(MH, MQ), L.take(MH, MQ)
        latT = L.take(3, P)
        rt, rt2 = L.take(MH, ROPE), L.take(MH, ROPE)
        qout = L.take(2 * HALF)
        wuq, wukv = L.take(2, MH * MQ), L.take(MH * P)
        rope = L.take(4 * NT, ROPE).rearrange("p (a t) r -> p a t r", a=4)
        pool_a, pool_b = flat(wreg, 0, (2, PAD + SEQ + PAD)), flat(wreg, 2 * 1040, (2, PAD + SEQ + PAD))
        invc = flat(wreg, 4 * 1040, (2, SEQ))
        wo = flat(wreg, 6400, (KD, D))
        bias = wreg[:, 6400 + KD * D:6400 + KD * D + DH * SEQ // 2].bitcast(F16).rearrange("p (h j) -> p h j", h=DH)
        L = Lay(work)
        qs = L.take(2 * HALF)
        SC = L.take(2, SEQ)
        E = L.take(4, SEQ)
        AT = L.take(NT, P)
        ob = L.take(DH * DV)
        om = L.take(MH * MV)
        osq = L.take(DH * DV)
        catT = L.take(KD, P)
        xt2 = L.take(D)
        hf = L.take(D)
        hT2 = catT
        junk2 = work[:, L.at:L.at + D // 2].bitcast(BF16)
        wr = sb("wr", [P, KD, NLOG])
        rs, rc, mn = sb("rs", [P, 12]), sb("rc", [P, 12]), sb("mn", [P, 12])
        cf = sb("cf", [P, DH])
        slot = [wreg[:, 0:SLOT], qreg[:, 0:SLOT], qreg[:, SLOT:2 * SLOT], wreg[:, SLOT:2 * SLOT]]
        L = Lay(work)
        G = L.take(2, D)
        gT = L.take(KD, CAP)
        sg, hh = L.take(2, CAP), L.take(2, CAP)
        Y = L.take(2, D)
        iota = L.take(SEQ + CAP)
        rank = L.take(NE + 2, NT)
        mb1, mb2 = L.take(NT, NE), L.take(NT, NE)
        big = L.take(NT, NE)
        gm_, ge_, gv_, gk_ = L.take(NT, NG), L.take(NT, NG), L.take(NT, NG), L.take(NT, NG)
        es, ev, ek1, ek2 = L.take(NT, EPG), L.take(NT, EPG), L.take(NT, EPG), L.take(NT, EPG)
        r8 = L.take(16, NT)
        eids = L.take(4, 2).bitcast(U32)
        OH = work[:, L.at:L.at + 768].bitcast(BF16).rearrange("p (r t s) -> p r t s", r=2, t=NT)
        L.at += 768
        n = (NE + 2) * NT * 3 // 2
        cols = work[:, L.at:L.at + n].bitcast(BF16).rearrange("p (e t c) -> p e t c", e=NE + 2, t=NT)
        L.at += n
        mb = work[:, L.at:L.at + P].bitcast(BF16).rearrange("p (t e) -> p t e", t=NT)
        L.at += P
        assert L.at <= WORK, L.at
        L = Lay(work)
        c_x, c_y = L.take(2, D), L.take(2, 2, D)

        PA = ctx.enter_context(nc.psum_tensor("PA", [P, HALF], F32))
        PB = ctx.enter_context(nc.psum_tensor("PB", [P, HALF], F32))
        PS = ctx.enter_context(nc.psum_tensor("PS", [P, 6 * HALF], F32))
        S = [PS[:, 0:SEQ], PS[:, SEQ:2 * SEQ]]
        OD = PS[:, 2 * SEQ:2 * SEQ + HALF].rearrange("p (h e) -> p h e", h=DH)
        OM = PS[:, 2 * SEQ + HALF:2 * SEQ + HALF + MH * MV].rearrange("p (h e) -> p h e", h=MH)
        GATE, UP = (PS[:, b * HALF:b * HALF + 2 * CAP].rearrange("p (f s) -> p f s", f=2) for b in range(2))
        DN = PS[0:CAP, SEQ:2 * SEQ]
        IDS = [PS[0:CAP, (4 + r) * HALF:(4 + r) * HALF + 3] for r in range(2)]

        ident = cst[:, K_ID:K_ID + P]
        NQS, NSUB, NLAM, MQS, X1 = 0, 1, 2, 3, 4

        names = [
            "phase_done", "carried", "consts_loaded", "x_copied", "small_ready", "lam_exp", "lam_sum", "step_dve", "step_pool",
            "win_loaded0", "x_loaded", "gain_loaded", "x_squared", "var_ready", "rstd_ready", "xn_ready",
            "ta_full", "ta_free", "tb_full", "tb_free", "proj_full", "proj_kept", "pj_normed", "mla_normed",
            "q_stored", "q_loaded", "bias_loaded", "wo_loaded", "x_stored", "h_stored",
            "scores_ready", "biased", "max_ready", "exp_done", "mixed", "pv_done",
            "od_ready", "om_ready", "pooled", "inv_loaded", "x_updated", "hf_ready",
            "iota_loaded", "wr_loaded", "weights_loaded", "route_exp", "route_arg", "mask_ready", "rank_full", "nmax_ready",
            "onehot_ready", "ids_full", "ids_ready", "gathered0", "gathered1", "gate_full", "up_full", "silu_ready",
            "h_ready", "down_full", "ya_ready", "yb_ready", "scattered0", "scattered1",
            "w0_loaded", "w1_loaded", "w2_loaded", "w3_loaded",
            "cx_loaded0", "cx_loaded1", "cx_ready", "cx_stored0", "cx_stored1",
            "o_w", "o_onehot", "o_ids", "o_conv", "o_g", "o_t", "o_ev", "o_gu", "o_silu", "o_h", "o_dn", "o_y",
            "o_s"]
        s = namedtuple("Semaphores", names)(*[sem(name) for name in names])
        wload = [s.w0_loaded, s.w1_loaded, s.w2_loaded, s.w3_loaded]
        gathered, scattered = [s.gathered0, s.gathered1], [s.scattered0, s.scattered1]
        cx_stored = [s.cx_stored0, s.cx_stored1]
        cx_loaded = [s.cx_loaded0, s.cx_loaded1]
        win_loaded = [s.win_loaded0] + [sem(f"win_loaded{k}") for k in range(1, KD)]

        T = NT - 1
        tok = lambda i: bass.ds(i * P, P)
        block = ctx.enter_context(nc.Block())

        def steady(eng):
            eng.sem_inc(s.carried, 1)

        def barrier(eng, phase):
            steady(eng)
            eng.drain().then_inc(s.phase_done, 1)
            eng.wait_ge(s.phase_done, phase.next(5))
            steady(eng)

        NB = NE * OVER

        @contextmanager
        def further_blocks(eng, layer, load_ready, raised):
            eng.wait_ge(s.nmax_ready, load_ready)
            steady(eng)
            most = eng.value_load(nmax[0:1, 0:1], min_val=0, max_val=SEQ)
            with eng.If(most > CAP):
                with eng.Fori(0, NE) as e:
                    with eng.Fori(0, OVER) as c:
                        yield e, c, layer * NB + e * OVER + c
            with eng.Else():
                for which, by in raised:
                    eng.sem_inc(which, NB * by)

        def overflow_tensor(pe, layer, ready, up_matmuls, down_matmuls):
            with further_blocks(pe, layer, ready, ((s.o_ids, 1), (s.o_t, 1), (s.o_gu, 1), (s.o_dn, 1))) as (e, c, b):
                pe.wait_ge(s.o_onehot, b + 1)
                for i in range(NT):
                    t = pe.matmul(IDS[0], OH[:, 0, i, :], cols[:, e, i, :], start=(i == 0), stop=(i == NT - 1))
                t.then_inc(s.o_ids, 1)
                pe.wait_ge(s.o_g, (b + 1) * 16)
                for bank, k0 in ((PA, 0), (PB, 4)):
                    for k in range(4):
                        t = pe.transpose(bank[:, k * CAP:(k + 1) * CAP],
                                         G[0:CAP, 0, (k0 + k) * P:(k0 + k + 1) * P], ident[0:CAP, 0:CAP])
                t.then_inc(s.o_t, 1)
                pe.wait_ge(s.o_ev, b + 1)
                pe.wait_ge(s.o_w, (b + 1) * 48)
                up_matmuls(slot[0][:, 0:KD * FF], GATE)
                up_matmuls(slot[0][:, KD * FF:2 * KD * FF], UP).then_inc(s.o_gu, 1)
                pe.wait_ge(s.o_h, b + 1)
                down_matmuls(slot[0][:, 2 * KD * FF:]).then_inc(s.o_dn, 1)

        def overflow_scalar(act, layer, ready):
            with further_blocks(act, layer, ready, ((s.o_silu, 1),)) as (e, c, b):
                act.wait_ge(s.o_gu, b + 1)
                act.activation(sg[:, :, :], GATE, ACT.Silu).then_inc(s.o_silu, 1)

        def overflow_vector(dve, layer, ready):
            raised = ((s.o_onehot, 1), (s.o_conv, 2), (s.o_ev, 2), (s.o_h, 1), (s.o_y, 2))
            with further_blocks(dve, layer, ready, raised) as (e, c, b):
                dve.tensor_tensor(OH[:, 0, :, :], iota[:, bass.ds((c + 1) * CAP, CAP)].unsqueeze(1).broadcast_to([P, NT, CAP]),
                                  rank[:, e, :].unsqueeze(2).broadcast_to([P, NT, CAP]),
                                  ALU.is_equal).then_inc(s.o_onehot, 1)
                dve.wait_ge(s.o_ids, b + 1)
                dve.wait_ge(s.o_s, b * 16)
                dve.tensor_reduce(eids[0:CAP, 0, 0:1], IDS[0][:, 0:2], AX.X, ALU.add).then_inc(s.o_conv, 1)
                dve.wait_ge(s.o_conv, b * 2 + 1)
                dve.scalar_tensor_tensor(eids[0:CAP, 0, 1:2], IDS[0][:, 2:3], float(OOB), eids[0:CAP, 0, 0:1],
                                         ALU.add, ALU.add).then_inc(s.o_conv, 1)
                dve.wait_ge(s.o_t, b + 1)
                dve.tensor_copy(gT[:, 0:4, :], PA[:, 0:4 * CAP].rearrange("p (k s) -> p k s", k=4)).then_inc(s.o_ev, 1)
                dve.tensor_copy(gT[:, 4:8, :], PB[:, 0:4 * CAP].rearrange("p (k s) -> p k s", k=4)).then_inc(s.o_ev, 1)
                dve.wait_ge(s.o_silu, b + 1)
                dve.tensor_tensor(hh[:, :, :], sg[:, :, :], UP, ALU.mult).then_inc(s.o_h, 1)
                dve.wait_ge(s.o_dn, b + 1)
                for half in range(2):
                    dve.tensor_copy(Y[0:CAP, 0, half * HALF:(half + 1) * HALF],
                                    DN[:, half * HALF:(half + 1) * HALF]).then_inc(s.o_y, 1)

        def overflow_gpsimd(pool, layer, ready):
            with further_blocks(pool, layer, ready, ((s.o_g, 16), (s.o_s, 16))) as (e, c, b):
                pool.wait_ge(s.o_conv, b * 2 + 2)
                gather_rows(pool, 0, 0).then_inc(s.o_g, 16)
                pool.wait_ge(s.o_y, b * 2 + 2)
                scatter_rows(pool, 0, 0).then_inc(s.o_s, 16)

        def overflow_sync(sp, layer, ready):
            with further_blocks(sp, layer, ready, ((s.o_w, 48),)) as (e, c, b):
                sp.wait_ge(s.o_s, b * 16)
                steady(sp)
                load_expert(sp, layer, e, 0, s.o_w)
            with sp.If(sp.value_load(nmax[0:1, 0:1], min_val=0, max_val=SEQ) > CAP):
                sp.wait_ge(s.o_s, (layer + 1) * (NB * 16))
                steady(sp)

        def load_expert(sp, layer, e, q, landed):
            w = slot[q]
            for src, at, k in ((w_gate, 0, KD), (w_up, KD * FF, KD), (w_down, 2 * KD * FF, 2)):
                n = FF if k == KD else D
                sp.dma_start(w[:, at:at + k * n].rearrange("p (k n) -> p k n", k=k),
                             src[layer, e].rearrange("(k p) n -> p k n", p=P)).then_inc(landed, 16)

        def gather_rows(pool, q, r):
            steady(pool)
            return pool.indirect_dma_start(out=G[0:CAP, r, :], out_offset=None, in_=h_dram[:, :],
                                           in_offset=bass.IndirectOffsetOnAxis(ap=eids[0:CAP, q, 0:1], axis=0),
                                           bounds_check=SEQ - 1, oob_is_err=False)

        def scatter_rows(pool, q, r):
            steady(pool)
            return pool.indirect_dma_start(out=y_dram[:, :],
                                           out_offset=bass.IndirectOffsetOnAxis(ap=eids[0:CAP, q, 1:2], axis=0),
                                           in_=Y[0:CAP, r, :], in_offset=None,
                                           bounds_check=2 * SEQ - 1, oob_is_err=False)

        @block.tensor
        def _(pe):
            n = Counts("pe")
            phase = n.on(s.phase_done, "phase")
            ta, tb = n.on(s.ta_free, "ta"), n.on(s.tb_free, "tb")
            xn, kept = n.on(s.xn_ready, "xn"), n.on(s.proj_kept, "kept")
            pjn, mln = n.on(s.pj_normed, "pjn"), n.on(s.mla_normed, "mln")
            win_c = n.on(s.win_loaded0, "win", 16)
            ql, wol = n.on(s.q_loaded, "ql", 16), n.on(s.wo_loaded, "wo", 16)
            biased, expd = n.on(s.biased, "biased"), n.on(s.exp_done, "exp")
            mixed, odr, omr = n.on(s.mixed, "mixed"), n.on(s.od_ready, "od"), n.on(s.om_ready, "om")
            pooled, hfr = n.on(s.pooled, "pooled"), n.on(s.hf_ready, "hf")
            masks, oh, gth = n.on(s.mask_ready, "mask"), n.on(s.onehot_ready, "oh"), [
                n.on(gathered[r], f"g{r}", 16) for r in range(2)]
            wl = [n.on(wload[r], f"w{r}", 16) for r in range(4)]
            hr, ya, yb = n.on(s.h_ready, "h"), n.on(s.ya_ready, "ya"), n.on(s.yb_ready, "yb")
            small_r, wrl, wtl = n.on(s.small_ready, "small"), n.on(s.wr_loaded, "wr", 16), n.on(s.weights_loaded, "wt", 16)

            def evacuated(c):
                pe.wait_ge(c.sem, c.value(c.k + 1))

            def turn(bank, src, w, rows=P, take=P):
                return pe.transpose(bank[0:w, 0:rows], src, ident[0:rows, 0:rows])

            def turn_x():
                pe.wait_ge(s.xn_ready, xn.next())
                for c, bank, full, k0 in ((ta, PA, s.ta_full, 0), (tb, PB, s.tb_full, 4)):
                    pe.wait_ge(c.sem, c.next())
                    for k in range(4):
                        t = pe.transpose(bank[:, k * P:(k + 1) * P], xn1[:, (k0 + k) * P:(k0 + k + 1) * P], ident)
                    t.then_inc(full, 1)

            def project(c, first=False):
                c0, w = CHUNKS[c]
                if not first:
                    pe.wait_ge(s.proj_kept, kept.next())
                for k in range(KD):
                    t = pe.matmul(PS[:, c * HALF:c * HALF + w], hT1[:, k, :], win[:, k, c0:c0 + w],
                                  start=(k == 0), stop=(k == KD - 1))
                t.then_inc(s.proj_full, 1)

            def project_first():
                win_c.next()
                for k in range(KD):
                    pe.wait_ge(win_loaded[k], win_c.last())
                    for c, (c0, w) in enumerate(CHUNKS):
                        t = pe.matmul(PS[:, c * HALF:c * HALF + w], hT1[:, k, :], win[:, k, c0:c0 + w],
                                      start=(k == 0), stop=(k == KD - 1))
                        if k == KD - 1:
                            t.then_inc(s.proj_full, 1)

            def turn_projected():
                pe.wait_ge(s.pj_normed, pjn.next())
                pe.wait_ge(s.ta_free, ta.next())
                for h in range(DH):
                    t = pe.transpose(PA[:, h * P:(h + 1) * P], pj[:, h * P:(h + 1) * P], ident)
                t.then_inc(s.ta_full, 1)
                pe.wait_ge(s.tb_free, tb.next())
                for h in range(DH):
                    t = pe.transpose(PB[:, h * P:(h + 1) * P], pj[:, HALF + h * P:HALF + (h + 1) * P], ident)
                t.then_inc(s.tb_full, 1)
                pe.wait_ge(s.tb_free, tb.next())
                for c in range(2):
                    t = pe.transpose(PB[:, c * P:(c + 1) * P], pj[:, O_PU + c * P:O_PU + (c + 1) * P], ident)
                t.then_inc(s.tb_full, 1)
                pe.wait_ge(s.ta_free, ta.next())
                pe.transpose(PA[:, 0:P], pj[:, O_LAT:O_LAT + P], ident)
                pe.transpose(PA[0:QR - P, P:2 * P], pj[:, O_LAT + P:O_LAT + QR], ident)
                pe.transpose(PA[:, 2 * P:3 * P], pj[:, O_LAT + QR:O_KR], ident).then_inc(s.ta_full, 1)

            def up_q():
                evacuated(ta)
                pe.wait_ge(s.tb_free, tb.next())
                pe.matmul(PB[:, 0:MH * MQ], latT[:, 0, :], wuq[:, 0, :], start=True, stop=False)
                pe.matmul(PB[:, 0:MH * MQ], latT[0:QR - P, 1, :], wuq[0:QR - P, 1, :],
                          start=False, stop=True).then_inc(s.tb_full, 1)

            def up_kv():
                pe.wait_ge(s.tb_free, tb.next())
                pe.matmul(PB[:, :], latT[:, 2, :], wukv[:, :], start=True, stop=True).then_inc(s.tb_full, 1)

            def turn_mla():
                pe.wait_ge(s.mla_normed, mln.next())
                for c, bank, full, src in ((ta, PA, s.ta_full, qc), (tb, PB, s.tb_full, kc)):
                    pe.wait_ge(c.sem, c.next())
                    for h in range(MH):
                        t = pe.transpose(bank[0:MQ, h * P:(h + 1) * P], src[:, h, :], ident)
                    t.then_inc(full, 1)

            def phase1():
                turn_x()
                evacuated(ta)
                evacuated(tb)
                project_first()
                turn_x()

                def body(last):
                    evacuated(ta)
                    evacuated(tb)
                    project(0)
                    turn_projected()
                    project(1)
                    up_q()
                    project(2)
                    up_kv()
                    project(3)
                    project(4)
                    turn_mla()
                    if not last:
                        turn_x()
                with n.loop(pe, "p1", 1, T):
                    body(False)
                body(True)
                turn_projected()
                up_q()
                up_kv()
                turn_mla()
                kept.next(5)

            def free_scores(m, c0, b0):
                if m in (10, 11):
                    pe.wait_ge(s.exp_done, expd.value(c0 + m - 1))
                elif 2 <= m < 10 or m in (14, 15):
                    pe.wait_ge(s.biased, biased.value(b0 + m - 1 if m < 10 else b0 + 8 + m - 13))
                elif m in (12, 13):
                    pe.wait_ge(s.exp_done, expd.value(c0 + m - 1))

            def scores(u, nxt=0):
                for m in ((2 * u, 2 * u + 1) if u < DH else (u + 4,)):
                    free_scores(m + nxt, expd.k, biased.k)
                    for half in range(2):
                        ks = slice(half * HALF, (half + 1) * HALF)
                        if u < DH:
                            r = slice(64 * (m % 2), 64 * (m % 2) + 64)
                            t = pe.matmul(S[m % 2][:, ks], qs[r, u * P:(u + 1) * P], kT[r, u, ks],
                                          start=True, stop=True)
                        else:
                            t = pe.matmul(S[m % 2][:, ks], qs[0:MQ, u * P:(u + 1) * P], kmT[0:MQ, u - DH, ks],
                                          start=True, stop=True)
                    t.then_inc(s.scores_ready, 1)

            def turn_probs(u):
                if u < DH:
                    pe.wait_ge(s.mixed, mixed.next())
                else:
                    pe.wait_ge(s.exp_done, expd.value(expd.k + u + 5))
                e = (2 * u) % 4 if u < DH else u - DH
                for c, bank, full, k0 in ((tb, PB, s.tb_full, 4), (ta, PA, s.ta_full, 0)):
                    pe.wait_ge(c.sem, c.next())
                    for k in range(4):
                        t = pe.transpose(bank[:, k * P:(k + 1) * P], E[:, e, (k0 + k) * P:(k0 + k + 1) * P], ident)
                    t.then_inc(full, 1)

            def values(u):
                evacuated(ta)
                evacuated(tb)
                o, v, w = (OD[:, u, :], V, DV) if u < DH else (OM[:, u - DH, :], VM, MV)
                c0 = (u % 4) * w
                for k in range(NT):
                    t = pe.matmul(o, AT[:, k, :], v[:, k, c0:c0 + w], start=(k == 0), stop=(k == NT - 1))
                t.then_inc(s.pv_done, 1)

            def route_tile():
                pe.wait_ge(s.hf_ready, hfr.next())
                for c, bank, full, k0 in ((tb, PB, s.tb_full, 4), (ta, PA, s.ta_full, 0)):
                    pe.wait_ge(c.sem, c.next())
                    for k in range(4):
                        t = pe.transpose(bank[:, k * P:(k + 1) * P], hf[:, (k0 + k) * P:(k0 + k + 1) * P], ident)
                    t.then_inc(full, 1)
                evacuated(ta)
                pe.wait_ge(s.tb_free, tb.next())
                for k in range(KD):
                    t = pe.matmul(PB[:, 0:NLOG], hT2[:, k, :], wr[:, k, :], start=(k == 0), stop=(k == KD - 1))
                t.then_inc(s.tb_full, 1)

            def turn_diff():
                pe.wait_ge(s.od_ready, odr.next())
                pe.wait_ge(s.ta_free, ta.next())
                for h in range(DH):
                    t = pe.transpose(PA[:, h * P:(h + 1) * P], ob[:, h * P:(h + 1) * P], ident)
                t.then_inc(s.ta_full, 1)

            def mix_pool(i, first):
                if first:
                    pe.wait_ge(s.pooled, pooled.next())
                pe.wait_ge(s.ta_free, ta.next())
                for c in range(2):
                    t = pe.matmul(PA[:, c * P:(c + 1) * P], pwd[:, c, :], put[:, c, bass.ds(i * P + PAD, P)],
                                  start=True, stop=True)
                t.then_inc(s.ta_full, 1)

            def turn_mla_out():
                pe.wait_ge(s.om_ready, omr.next())
                pe.wait_ge(s.tb_free, tb.next())
                for c in range(2):
                    t = pe.transpose(PB[:, c * P:(c + 1) * P], om[:, c * P:(c + 1) * P], ident)
                t.then_inc(s.tb_full, 1)

            def project_out():
                evacuated(ta)
                for half in range(2):
                    pe.wait_ge(s.tb_free, tb.next())
                    for k in range(KD):
                        t = pe.matmul(PB[:, :], catT[:, k, :], wo[:, k, half * HALF:(half + 1) * HALF],
                                      start=(k == 0), stop=(k == KD - 1))
                    t.then_inc(s.tb_full, 1)

            def phase2():
                def body(i, first, last):
                    for u in range(8):
                        turn_probs(u)
                        if u <= 5:
                            scores(u + 2)
                        if u == 7 and not last:
                            pe.wait_ge(s.q_loaded, ql.next())
                            scores(0, 12)
                        values(u)
                        if u == 2 and not first:
                            route_tile()
                        if u == 6:
                            turn_diff()
                    if not last:
                        scores(1, 12)
                    mix_pool(i, first)
                    turn_mla_out()
                    if first:
                        pe.wait_ge(s.wo_loaded, wol.next())
                    project_out()
                    biased.next(8)
                    expd.next(12)

                pe.wait_ge(s.wr_loaded, wrl.next())
                pe.wait_ge(s.q_loaded, ql.next())
                scores(0)
                scores(1)
                body(0, True, False)
                with n.loop(pe, "p2", 1, T) as i:
                    body(i, False, False)
                body(T, False, True)
                route_tile()

            def rank_tokens():
                pe.wait_ge(s.mask_ready, masks.next())
                for i in range(NT):
                    for j in range(i + 1):
                        pe.matmul(PS[:, i * NE:(i + 1) * NE], tri[:, :] if j == i else ones[:, :], mb[:, j, :],
                                  start=(j == 0), stop=(j == i))
                for j in range(NT):
                    t = pe.matmul(PS[:, NT * NE:(NT + 1) * NE], ones[:, :], mb[:, j, :],
                                  start=(j == 0), stop=(j == NT - 1))
                t.then_inc(s.rank_full, 1)

            def slot_ids(e, r):
                pe.wait_ge(s.onehot_ready, oh.next())
                for i in range(NT):
                    t = pe.matmul(IDS[r], OH[:, r, i, :], cols[:, e, i, :], start=(i == 0), stop=(i == NT - 1))
                t.then_inc(s.ids_full, 1)

            def turn_rows(r):
                pe.wait_ge(gathered[r], gth[r].next())
                for c, bank, full, k0 in ((ta, PA, s.ta_full, 0), (tb, PB, s.tb_full, 4)):
                    pe.wait_ge(c.sem, c.next())
                    for k in range(4):
                        t = pe.transpose(bank[:, k * CAP:(k + 1) * CAP],
                                         G[0:CAP, r, (k0 + k) * P:(k0 + k + 1) * P], ident[0:CAP, 0:CAP])
                    t.then_inc(full, 1)

            def up_matmuls(w, bank):
                for f in range(2):
                    for k in range(KD):
                        t = pe.matmul(bank[:, f, :], w[:, k * FF + f * P:k * FF + (f + 1) * P], gT[:, k, :],
                                      start=(k == 0), stop=(k == KD - 1))
                return t

            def down_matmuls(w):
                for half in range(2):
                    for f in range(2):
                        t = pe.matmul(DN[:, half * HALF:(half + 1) * HALF], hh[:, f, :],
                                      w[:, f * D + half * HALF:f * D + (half + 1) * HALF],
                                      start=(f == 0), stop=(f == 1))
                return t

            def phase3():
                rank_tokens()
                slot_ids(0, 0)
                slot_ids(1, 1)
                turn_rows(0)
                with n.loop(pe, "p3", 0, NE // 4) as j:
                    for q in range(4):
                        r = q % 2
                        w = slot[q]
                        evacuated(ta)
                        evacuated(tb)
                        pe.wait_ge(wload[q], wl[q].next(3))
                        up_matmuls(w[:, 0:KD * FF], GATE).then_inc(s.gate_full, 1)
                        up_matmuls(w[:, KD * FF:2 * KD * FF], UP).then_inc(s.up_full, 1)
                        slot_ids(j * 4 + (q + 2), r)
                        turn_rows(1 - r)
                        pe.wait_ge(s.h_ready, hr.next())
                        pe.wait_ge(s.ya_ready, ya.next())
                        pe.wait_ge(s.yb_ready, yb.next())
                        down_matmuls(w[:, 2 * KD * FF:]).then_inc(s.down_full, 1)
                gth[1].next()

            pe.wait_ge(s.consts_loaded, 36)
            with pe.Fori(0, DEPTH) as layer:
                n.enter_layer(layer)
                pe.wait_ge(s.small_ready, small_r.next())
                pe.wait_ge(s.weights_loaded, wtl.next(4))
                phase1()
                barrier(pe, phase)
                phase2()
                barrier(pe, phase)
                phase3()
                barrier(pe, phase)
                overflow_tensor(pe, layer, layer + 1, up_matmuls, down_matmuls)
                barrier(pe, phase)
                n.leave_layer()

        @block.scalar
        def _(act):
            n = Counts("act")
            phase = n.on(s.phase_done, "phase")
            ta, mine, tb = n.on(s.ta_full, "ta"), n.on(s.ta_free, "mine"), n.on(s.tb_full, "tb")
            xl, pf, pjn = n.on(s.x_loaded, "x", 16), n.on(s.proj_full, "pf"), n.on(s.pj_normed, "pjn")
            qst = n.on(s.q_stored, "qst", 16)
            biased, maxr, xup = n.on(s.biased, "biased"), n.on(s.max_ready, "max"), n.on(s.x_updated, "xup")
            rarg, lam = n.on(s.route_arg, "rarg"), n.on(s.lam_sum, "lam")
            gf, dn = n.on(s.gate_full, "gf"), n.on(s.down_full, "dn")
            sct = [n.on(scattered[r], f"s{r}", 16) for r in range(2)]
            cxr, cxs = n.on(s.cx_ready, "cxr"), [n.on(cx_stored[r], f"cxs{r}", 16) for r in range(2)]
            small_r = n.on(s.small_ready, "small")

            def scaled(out_, in_, scale):
                return act.activation(out_, in_, ACT.Copy, scale=scale)

            def square_x():
                act.wait_ge(s.x_loaded, xl.next())
                act.activation(junk1, xt1, ACT.Square, accum_out=st[:, 0, 20:21]).then_inc(s.x_squared, 1)

            def keep_x():
                act.wait_ge(s.ta_full, ta.next())
                act.copy(hT1[:, 0:4, :], PA[:, :].rearrange("p (k t) -> p k t", k=4)).then_inc(s.ta_free, 1)
                mine.next()

            def keep_projected(i, first, only=None):
                for c in range(5) if only is None else only:
                    act.wait_ge(s.proj_full, pf.next())
                    w = CHUNKS[c][1]
                    dst = (pj[:, 0:HALF], pj[:, HALF:2 * HALF], V[:, i, :], pj[:, O_LAT:O_LAT + 352],
                           pj[:, O_PU:PJ])[c]
                    act.copy(dst, PS[:, c * HALF:c * HALF + w]).then_inc(s.proj_kept, 1)

            def keep_turned():
                act.wait_ge(s.ta_full, ta.next())
                act.wait_ge(s.q_stored, qst.last())
                scaled(qout[:, 0:HALF], PA[:, :], der[:, NQS:NQS + 1]).then_inc(s.ta_free, 1)
                mine.next()
                act.wait_ge(s.ta_full, ta.next())
                scaled(latT[:, 0, :], PA[:, 0:P], cur[:, C_QL:C_QL + 1])
                scaled(latT[0:QR - P, 1, :], PA[0:QR - P, P:2 * P], cur[0:QR - P, C_QL + 1:C_QL + 2])
                scaled(latT[:, 2, :], PA[:, 2 * P:3 * P], cur[:, C_KVL:C_KVL + 1]).then_inc(s.ta_free, 1)
                mine.next()

            def keep_mla(i):
                act.wait_ge(s.ta_full, ta.next())
                scaled(qout[0:MQ, HALF:2 * HALF], PA[0:MQ, :], der[0:MQ, MQS:MQS + 1]).then_inc(s.ta_free, 1)
                act.wait_ge(s.ta_free, mine.next() + 1)
                act.dma_start(q_dram[i], qout).then_inc(s.q_stored, 16)
                qst.next()

            def phase1():
                act.wait_ge(s.lam_sum, lam.next())
                act.activation(der[:, X1 + 2:X1 + 4], der[:, X1:X1 + 2], ACT.Exp).then_inc(s.lam_exp, 1)
                act.wait_ge(s.small_ready, small_r.next())
                square_x()
                keep_x()
                square_x()
                keep_projected(0, True)
                keep_x()

                def body(i, last):
                    keep_projected_after_turn(i)
                    keep_projected(i, False, (1, 2, 3, 4))
                    if not last:
                        square_x()
                    keep_mla(i - 1)
                    if not last:
                        keep_x()

                def keep_projected_after_turn(i):
                    keep_turned()
                    keep_projected(i, False, (0,))
                with n.loop(act, "p1", 1, T) as i:
                    body(i, False)
                body(T, True)
                keep_turned()
                keep_mla(T)
                act.wait_ge(s.q_stored, qst.last())
                xl.next(NT)

            def exponents(u, b0):
                for m in ((2 * u, 2 * u + 1) if u < DH else (u + 4,)):
                    if u < DH:
                        act.wait_ge(s.biased, biased.value(b0 + m + 1))
                        act.activation(E[:, m % 4, :], SC[:, m % 2, :], ACT.Exp, scale=-1.0,
                                       bias=mn[:, m:m + 1], accum_out=rs[:, m:m + 1]).then_inc(s.exp_done, 1)
                    else:
                        act.wait_ge(s.max_ready, maxr.next())
                        act.activation(E[:, m % 4, :], S[m % 2], ACT.Exp, bias=mn[:, m:m + 1],
                                       accum_out=rs[:, m:m + 1]).then_inc(s.exp_done, 1)

            def keep_left(dst):
                act.wait_ge(s.ta_full, ta.next())
                act.copy(dst[:, 0:4, :], PA[:, :].rearrange("p (k t) -> p k t", k=4)).then_inc(s.ta_free, 1)
                mine.next()

            def phase2():
                def body(first, last):
                    for u in range(8):
                        keep_left(AT)
                        if u <= 5:
                            exponents(u + 2, biased.k)
                        if u == 7 and not last:
                            exponents(0, biased.k + 8)
                        if u == 2 and not first:
                            keep_left(hT2)
                        if u == 6:
                            act.wait_ge(s.ta_full, ta.next())
                            scaled(catT[:, 0:4, :], PA[:, :].rearrange("p (k t) -> p k t", k=4),
                                   der[:, NSUB:NSUB + 1]).then_inc(s.ta_free, 1)
                            mine.next()
                    if not last:
                        exponents(1, biased.k + 8)
                    act.wait_ge(s.ta_full, ta.next())
                    scaled(catT[:, 6, :], PA[:, 0:P], cur[:, C_PS:C_PS + 1])
                    scaled(catT[:, 7, :], PA[:, P:2 * P], cur[:, C_PS + 1:C_PS + 2]).then_inc(s.ta_free, 1)
                    mine.next()
                    act.wait_ge(s.x_updated, xup.next(2))
                    act.activation(junk2[:, :], xt2, ACT.Square, accum_out=st[:, 0, 20:21]).then_inc(s.x_squared, 1)
                    biased.next(8)

                exponents(0, 0)
                exponents(1, 0)
                body(True, False)
                with n.loop(act, "p2", 1, T):
                    body(False, False)
                body(False, True)
                keep_left(hT2)

            def phase3():
                act.wait_ge(s.route_arg, rarg.next())
                act.activation(ge_[:, :, :], gv_[:, :, :], ACT.Exp).then_inc(s.route_exp, 1)
                act.wait_ge(s.route_arg, rarg.next())
                act.activation(r8[:, 5, :], r8[:, 4, :], ACT.Exp).then_inc(s.route_exp, 1)

                def keep_rows():
                    act.wait_ge(s.ta_full, ta.next())
                    act.copy(gT[:, 0:4, :], PA[:, 0:4 * CAP].rearrange("p (k t) -> p k t", k=4)).then_inc(s.ta_free, 1)
                    mine.next()
                keep_rows()
                with n.loop(act, "p3", 0, NE // 4):
                    for q in range(4):
                        r = q % 2
                        act.wait_ge(s.gate_full, gf.next())
                        act.activation(sg[:, :, :], GATE, ACT.Silu).then_inc(s.silu_ready, 1)
                        keep_rows()
                        act.wait_ge(s.down_full, dn.next())
                        act.wait_ge(scattered[r], sct[r].last())
                        sct[r].next()
                        act.copy(Y[0:CAP, r, 0:HALF], DN[:, 0:HALF]).then_inc(s.ya_ready, 1)

            def phase4():
                with n.loop(act, "p4", 0, NT // 2) as j:
                    for r in range(2):
                        act.wait_ge(s.cx_ready, cxr.next(2))
                        act.dma_start(xs[tok(j * 2 + r), :], c_x[:, r, :]).then_inc(cx_stored[r], 16)
                        cxs[r].next()
                for r in range(2):
                    act.wait_ge(cx_stored[r], cxs[r].last())

            act.sem_inc(s.ta_free, 1)
            act.sem_inc(s.ya_ready, 1)
            act.wait_ge(s.consts_loaded, 36)
            with act.Fori(0, DEPTH) as layer:
                n.enter_layer(layer)
                phase1()
                barrier(act, phase)
                phase2()
                barrier(act, phase)
                phase3()
                barrier(act, phase)
                overflow_scalar(act, layer, layer + 1)
                phase4()
                barrier(act, phase)
                n.leave_layer()

        @block.vector
        def _(dve):
            n = Counts("dve")
            phase, step = n.on(s.phase_done, "phase"), n.on(s.step_dve, "step")
            tb, mine = n.on(s.tb_full, "tb"), n.on(s.tb_free, "mine")
            xsq, rstd, kept = n.on(s.x_squared, "xsq"), n.on(s.rstd_ready, "rstd"), n.on(s.proj_kept, "kept")
            gl, bl, lamx = n.on(s.gain_loaded, "gl", 16), n.on(s.bias_loaded, "bl", 16), n.on(s.lam_exp, "lamx")
            sr, expd, pv = n.on(s.scores_ready, "sr"), n.on(s.exp_done, "exp"), n.on(s.pv_done, "pv")
            xl, xst, hst = n.on(s.x_loaded, "x", 16), n.on(s.x_stored, "xst", 16), n.on(s.h_stored, "hst", 16)
            iol, rex = n.on(s.iota_loaded, "iota", 16), n.on(s.route_exp, "rex")
            rankf, idf = n.on(s.rank_full, "rank"), n.on(s.ids_full, "ids")
            silu, upf, dn = n.on(s.silu_ready, "silu"), n.on(s.up_full, "up"), n.on(s.down_full, "dn")
            sct = [n.on(scattered[r], f"s{r}", 16) for r in range(2)]
            cxl = [n.on(cx_loaded[r], f"cx{r}", 16) for r in range(2)]
            cxr, smr = n.on(s.cx_ready, "cxr"), n.on(s.small_ready, "small")

            def do(ins):
                ins.then_inc(s.step_dve, 1)
                step.next()

            def settle():
                dve.wait_ge(s.step_dve, step.last())

            def keep(dst, src, scale=None, after=None):
                dve.wait_ge(s.tb_full, tb.next())
                if scale is None:
                    t = dve.tensor_copy(dst, src)
                else:
                    t = dve.tensor_scalar(dst, src, scale, None, ALU.mult)
                t.then_inc(s.tb_free, 1)
                mine.next()

            def bc(a, w):
                return a.unsqueeze(2).broadcast_to([a.shape[0], a.shape[1], w])

            def over(a, m):
                return a.unsqueeze(1).broadcast_to([a.shape[0], m, a.shape[1]])

            def rsqrt_asked(t):
                t.then_inc(s.var_ready, 1)
                dve.wait_ge(s.rstd_ready, rstd.next())

            def set_up_layer(layer):
                do(dve.tensor_copy(cur[:, :], sm[:, layer, :]))
                settle()
                do(dve.tensor_scalar(der[:, NQS:NQS + 1], cur[:, C_DQG:C_DQG + 1], -(DQ ** -0.5), None, ALU.mult))
                do(dve.tensor_scalar(der[:, MQS:MQS + 1], cur[:, C_MQG:C_MQG + 1], MQ ** -0.5, None, ALU.mult))
                do(dve.tensor_tensor(der[:, NSUB:NSUB + 1], cur[:, C_SUB:C_SUB + 1], cur[:, C_LI + 1:C_LI + 2], ALU.mult))
                lv = cur[:, C_LAM:C_LAM + 4 * DQ].rearrange("p (a b d) -> p a b d", a=2, b=2)
                do(dve.tensor_tensor(rt.rearrange("p h r -> p (h r)").rearrange("p (a d) -> p a d", a=2),
                                     lv[:, :, 0, :], lv[:, :, 1, :], ALU.mult))
                settle()
                dve.tensor_reduce(der[:, X1:X1 + 2], rt.rearrange("p h r -> p (h r)").rearrange("p (a d) -> p a d", a=2),
                                  AX.X, ALU.add).then_inc(s.lam_sum, 1)
                dve.wait_ge(s.lam_exp, lamx.next())
                do(dve.tensor_tensor(der[:, X1 + 4:X1 + 5], der[:, X1 + 3:X1 + 4], der[:, X1 + 2:X1 + 3], ALU.subtract))
                settle()
                do(dve.tensor_tensor(der[:, NLAM:NLAM + 1], der[:, X1 + 4:X1 + 5], cur[:, C_LI:C_LI + 1], ALU.subtract))
                for t, (k, c) in enumerate(((K_COS, C_RGQ), (K_SIN, C_RSQ), (K_COS, C_RGK), (K_SIN, C_RSK))):
                    table = dve.tensor_tensor(rope[:, t, :, :], cst[:, k:k + NT * ROPE].rearrange("p (t r) -> p t r", t=NT),
                                              over(cur[:, c:c + ROPE], NT), ALU.mult)
                    if t < 3:
                        do(table)
                        settle()
                table.then_inc(s.small_ready, 1)
                dve.wait_ge(s.small_ready, smr.next())

            def norm_x(first=False):
                dve.wait_ge(s.x_squared, xsq.next())
                rsqrt_asked(dve.tensor_scalar(st[:, 1, 20:21], st[:, 0, 20:21], 1.0 / D, EPS, ALU.mult, ALU.add))
                if first:
                    dve.wait_ge(s.gain_loaded, gl.next())
                dve.scalar_tensor_tensor(xn1, xt1, st[:, 2, 20:21], grow[:, :], ALU.mult, ALU.mult).then_inc(s.xn_ready, 1)

            def keep_x():
                keep(hT1[:, 4:8, :], PB[:, :].rearrange("p (k t) -> p k t", k=4))

            def keep_turned(i):
                keep(kT[:, :, tok(i)], PB[:, :].rearrange("p (h t) -> p h t", h=DH), cur[:, C_DKG:C_DKG + 1])
                keep(put[:, :, bass.ds(i * P + PAD, P)], PB[:, 0:2 * P].rearrange("p (c t) -> p c t", c=2))

            def norm_projected(i):
                dve.wait_ge(s.proj_kept, kept.next(5))
                do(dve.tensor_tensor(sq, pj[:, 0:O_PU], pj[:, 0:O_PU], ALU.mult))
                settle()
                for c0, c1, a, g in ((0, O_LAT, 0, 16), (O_LAT, O_LAT + QR, 16, 1), (O_LAT + QR, O_KR, 17, 1),
                                     (O_KR, O_PU, 18, 1)):
                    do(dve.tensor_reduce(st[:, 0, a:a + g], sq[:, c0:c1].rearrange("p (g d) -> p g d", g=g),
                                         AX.X, ALU.add))
                settle()
                do(dve.tensor_tensor(st[:, 0, 0:NSTAT], st[:, 0, 0:NSTAT], cst[:, K_INV:K_INV + NSTAT], ALU.mult))
                settle()
                rsqrt_asked(dve.tensor_scalar(st[:, 1, 0:NSTAT], st[:, 0, 0:NSTAT], EPS, None, ALU.add))
                v = pj[:, 0:O_LAT].rearrange("p (g d) -> p g d", g=16)
                do(dve.tensor_tensor(v, v, bc(st[:, 2, 0:16], DQ), ALU.mult))
                for c0, c1, a in ((O_LAT, O_LAT + QR, 16), (O_LAT + QR, O_KR, 17), (O_KR, O_PU, 18)):
                    do(dve.tensor_scalar(pj[:, c0:c1], pj[:, c0:c1], st[:, 2, a:a + 1], None, ALU.mult))
                settle()
                kr = pj[:, O_KR:O_PU]
                do(dve.tensor_tensor(rt[:, 0, :], kr, rope[:, 2, i, :], ALU.mult))
                do(dve.tensor_tensor(rt2[:, 0, 0:16], kr[:, 16:32], rope[:, 3, i, 0:16], ALU.mult))
                do(dve.tensor_tensor(rt2[:, 0, 16:32], kr[:, 0:16], rope[:, 3, i, 16:32], ALU.mult))
                settle()
                dve.tensor_tensor(kc[:, :, NOPE:MQ], over(rt[:, 0, :], MH), over(rt2[:, 0, :], MH),
                                  ALU.add).then_inc(s.pj_normed, 1)

            def norm_mla(i):
                dve.wait_ge(s.tb_free, mine.last() + 1)
                nq = MH * MQ
                do(dve.tensor_tensor(sq[:, 0:nq + HALF], mj, mj, ALU.mult))
                q, k = mj[:, 0:nq].rearrange("p (h d) -> p h d", h=MH), mj[:, nq:].rearrange("p (h d) -> p h d", h=MH)
                q2, k2 = (sq[:, 0:nq].rearrange("p (h d) -> p h d", h=MH),
                          sq[:, nq:nq + HALF].rearrange("p (h d) -> p h d", h=MH))
                do(dve.tensor_copy(VM[:, i, :].rearrange("p (h d) -> p h d", h=MH), k[:, :, NOPE:NOPE + MV]))
                settle()
                do(dve.tensor_reduce(st[:, 0, 0:4], q2[:, :, 0:NOPE], AX.X, ALU.add))
                do(dve.tensor_reduce(st[:, 0, 4:8], q2[:, :, NOPE:MQ], AX.X, ALU.add))
                do(dve.tensor_reduce(st[:, 0, 8:12], k2[:, :, 0:NOPE], AX.X, ALU.add))
                settle()
                do(dve.tensor_tensor(st[:, 0, 0:12], st[:, 0, 0:12], cst[:, K_INV2:K_INV2 + 12], ALU.mult))
                settle()
                rsqrt_asked(dve.tensor_scalar(st[:, 1, 0:12], st[:, 0, 0:12], EPS, None, ALU.add))
                do(dve.tensor_tensor(qc[:, :, 0:NOPE], q[:, :, 0:NOPE], bc(st[:, 2, 0:4], NOPE), ALU.mult))
                do(dve.tensor_tensor(kc[:, :, 0:NOPE], k[:, :, 0:NOPE], bc(st[:, 2, 8:12], NOPE), ALU.mult))
                do(dve.tensor_tensor(q[:, :, NOPE:MQ], q[:, :, NOPE:MQ], bc(st[:, 2, 4:8], ROPE), ALU.mult))
                settle()
                do(dve.tensor_tensor(rt[:, :, :], q[:, :, NOPE:MQ], over(rope[:, 0, i, :], MH), ALU.mult))
                do(dve.tensor_tensor(rt2[:, :, 0:16], q[:, :, NOPE + 16:MQ], over(rope[:, 1, i, 0:16], MH), ALU.mult))
                do(dve.tensor_tensor(rt2[:, :, 16:32], q[:, :, NOPE:NOPE + 16], over(rope[:, 1, i, 16:32], MH), ALU.mult))
                settle()
                dve.tensor_tensor(qc[:, :, NOPE:MQ], rt[:, :, :], rt2[:, :, :], ALU.add).then_inc(s.mla_normed, 1)

            def keep_mla_in():
                keep(mj[:, 0:MH * MQ], PB[:, 0:MH * MQ])
                keep(mj[:, MH * MQ:], PB[:, :])

            def keep_mla(i):
                keep(kmT[0:MQ, :, tok(i)], PB[0:MQ, :].rearrange("p (h t) -> p h t", h=MH), cur[0:MQ, C_MKG:C_MKG + 1])

            def phase1():
                norm_x(True)
                keep_x()
                norm_x()
                keep_x()
                norm_projected(0)

                def body(i, last):
                    keep_turned(i - 1)
                    keep_mla_in()
                    norm_mla(i - 1)
                    if not last:
                        norm_x()
                    keep_mla(i - 1)
                    if not last:
                        keep_x()
                    norm_projected(i)
                with n.loop(dve, "p1", 1, T) as i:
                    body(i, False)
                body(T, True)
                keep_turned(T)
                keep_mla_in()
                norm_mla(T)
                keep_mla(T)

            def bias_scores(u, c0, nxt=0):
                if u == 0:
                    dve.wait_ge(s.bias_loaded, bl.next())
                for m in ((2 * u, 2 * u + 1) if u < DH else (u + 4,)):
                    dve.wait_ge(s.scores_ready, sr.next())
                    if u < DH:
                        if m >= 2:
                            dve.wait_ge(s.exp_done, expd.value(c0 + nxt + m - 1))
                        steady(dve)
                        dve.tensor_tensor_reduce(SC[:, m % 2, :], S[m % 2], bias[:, u, :],
                                                 1.0, 3.0e38, ALU.add, ALU.min, mn[:, m:m + 1]).then_inc(s.biased, 1)
                    else:
                        dve.tensor_reduce(mn[:, m:m + 1], S[m % 2], AX.X, ALU.max, negate=True).then_inc(s.max_ready, 1)

            def mix(u, c0, nxt=0):
                if u < DH:
                    dve.wait_ge(s.exp_done, expd.value(c0 + nxt + 2 * u + 2))
                    do(dve.reciprocal(rc[:, 2 * u:2 * u + 2], rs[:, 2 * u:2 * u + 2]))
                    settle()
                    do(dve.tensor_scalar(cf[:, u:u + 1], rs[:, 2 * u:2 * u + 1], rc[:, 2 * u + 1:2 * u + 2],
                                         der[:, NLAM:NLAM + 1], ALU.mult, ALU.mult))
                    settle()
                    e = (2 * u) % 4
                    dve.scalar_tensor_tensor(E[:, e, :], E[:, e + 1, :], cf[:, u:u + 1], E[:, e, :],
                                             ALU.mult, ALU.add).then_inc(s.mixed, 1)
                else:
                    dve.wait_ge(s.exp_done, expd.value(c0 + nxt + u + 5))
                    do(dve.reciprocal(rc[:, u + 4:u + 5], rs[:, u + 4:u + 5]))

            def keep_right(dst):
                keep(dst[:, 4:8, :], PB[:, :].rearrange("p (k t) -> p k t", k=4))

            def variance_x():
                dve.wait_ge(s.x_squared, xsq.next())
                dve.tensor_scalar(st[:, 1, 20:21], st[:, 0, 20:21], 1.0 / D, EPS, ALU.mult, ALU.add).then_inc(s.var_ready, 1)

            def norm_x2(second=False):
                dve.wait_ge(s.rstd_ready, rstd.next())
                if second:
                    dve.wait_ge(s.gain_loaded, gl.next())
                dve.wait_ge(s.h_stored, hst.last())
                hst.next()
                dve.scalar_tensor_tensor(hf, xt2, st[:, 2, 20:21], grow[:, :], ALU.mult, ALU.mult).then_inc(s.hf_ready, 1)

            def keep_routed(i):
                keep_right(hT2)
                dve.wait_ge(s.tb_full, tb.next())
                dve.tensor_tensor(logits[:, i, :], PB[:, 0:NLOG], cur[:, C_RB:C_RB + NLOG], ALU.add).then_inc(s.tb_free, 1)
                mine.next()

            def norm_diff_start():
                dve.wait_ge(s.pv_done, pv.value(pv.k + 4))
                o3, q3 = ob.rearrange("p (h d) -> p h d", h=DH), osq.rearrange("p (h d) -> p h d", h=DH)
                do(dve.tensor_tensor(o3, OD, bc(rc[:, 0:8:2], DV), ALU.mult))
                settle()
                do(dve.tensor_tensor(q3, o3, o3, ALU.mult))
                settle()
                do(dve.tensor_reduce(st[:, 0, 12:16], q3, AX.X, ALU.add))
                settle()
                dve.tensor_scalar(st[:, 1, 12:16], st[:, 0, 12:16], 1.0 / DV, EPS, ALU.mult, ALU.add).then_inc(s.var_ready, 1)

            def norm_diff_end():
                dve.wait_ge(s.rstd_ready, rstd.next())
                o3 = ob.rearrange("p (h d) -> p h d", h=DH)
                dve.tensor_tensor(o3, o3, bc(st[:, 2, 12:16], DV), ALU.mult).then_inc(s.od_ready, 1)

            def phase2():
                def body(i, first, last):
                    c0 = expd.k
                    for u in range(8):
                        keep_right(AT)
                        if u <= 6:
                            mix(u + 1, c0)
                        if u <= 5:
                            bias_scores(u + 2, c0)
                        if u == 7 and not last:
                            bias_scores(0, c0, 12)
                        if not first:
                            if u == 0:
                                variance_x()
                            if u == 1:
                                norm_x2(False)
                            if u == 2:
                                keep_routed(i - 1)
                        if u == 4:
                            norm_diff_start()
                        if u == 5:
                            norm_diff_end()
                    dve.wait_ge(s.pv_done, pv.next(8))
                    settle()
                    dve.tensor_tensor(om.rearrange("p (h d) -> p h d", h=MH), OM, bc(rc[:, 8:12], MV),
                                      ALU.mult).then_inc(s.om_ready, 1)
                    if not last:
                        bias_scores(1, c0, 12)
                        mix(0, c0, 12)
                    keep(catT[:, 4:6, :], PB[:, 0:2 * P].rearrange("p (c t) -> p c t", c=2))
                    dve.wait_ge(s.x_loaded, xl.next())
                    for half in range(2):
                        ks = slice(half * HALF, (half + 1) * HALF)
                        dve.wait_ge(s.tb_full, tb.next())
                        dve.tensor_tensor(xt2[:, ks], PB[:, :], xt2[:, ks], ALU.add).then_inc(s.x_updated, 1)
                        dve.wait_ge(s.x_updated, xup.next())
                        dve.sem_inc(s.tb_free, 1)
                        mine.next()
                    expd.next(12)

                xl.next(NT)
                bias_scores(0, 0)
                bias_scores(1, 0)
                mix(0, 0)
                body(0, True, False)
                dve.wait_ge(s.gain_loaded, gl.next())
                steady(dve)
                with n.loop(dve, "p2", 1, T) as i:
                    body(i, False, False)
                body(T, False, True)
                variance_x()
                norm_x2()
                keep_routed(T)

            xup = n.on(s.x_updated, "xup")

            def least_index(mask, val, values, best, w):
                do(dve.tensor_tensor(mask, values, bc(best, w), ALU.is_equal))
                settle()
                i8 = cst[:, K_I8:K_I8 + w].unsqueeze(1).broadcast_to([P, NT, w])
                do(dve.scalar_tensor_tensor(val, mask, -16.0, i8, ALU.mult, ALU.add))
                settle()
                do(dve.tensor_reduce(r8[:, 15, :], val, AX.X, ALU.min))
                settle()
                do(dve.tensor_tensor(mask, val, bc(r8[:, 15, :], w), ALU.is_equal))
                settle()

            def route():
                settle()
                dve.wait_ge(s.tb_free, mine.last() + 1)
                GL, EL = logits[:, :, 0:NG], logits[:, :, NG:NLOG]
                do(dve.tensor_reduce(r8[:, 0, :], GL, AX.X, ALU.max))
                settle()
                dve.tensor_tensor(gv_, GL, bc(r8[:, 0, :], NG), ALU.subtract).then_inc(s.route_arg, 1)
                least_index(gm_, gk_, GL, r8[:, 0, :], NG)
                dve.wait_ge(s.route_exp, rex.next())
                do(dve.tensor_reduce(r8[:, 1, :], ge_, AX.X, ALU.add))
                m4 = mb1.rearrange("p t (g e) -> p t g e", g=NG)
                do(dve.tensor_tensor(m4, EL.rearrange("p t (g e) -> p t g e", g=NG),
                                     gm_.unsqueeze(3).broadcast_to([P, NT, NG, EPG]), ALU.mult))
                settle()
                do(dve.tensor_reduce(es, mb1.rearrange("p t (g e) -> p t e g", g=NG), AX.X, ALU.add))
                settle()
                do(dve.tensor_reduce(r8[:, 2, :], es, AX.X, ALU.max))
                settle()
                least_index(ek1, ev, es, r8[:, 2, :], EPG)
                do(dve.scalar_tensor_tensor(es, ek1, -1.0e30, es, ALU.mult, ALU.add))
                settle()
                do(dve.tensor_reduce(r8[:, 3, :], es, AX.X, ALU.max))
                settle()
                dve.tensor_tensor(r8[:, 4, :], r8[:, 3, :], r8[:, 2, :], ALU.subtract).then_inc(s.route_arg, 1)
                least_index(ek2, ev, es, r8[:, 3, :], EPG)
                g4 = gm_.unsqueeze(3).broadcast_to([P, NT, NG, EPG])
                for m, ek in ((mb1, ek1), (mb2, ek2)):
                    do(dve.tensor_tensor(m.rearrange("p t (g e) -> p t g e", g=NG), g4,
                                         ek.unsqueeze(2).broadcast_to([P, NT, NG, EPG]), ALU.mult))
                settle()
                do(dve.tensor_tensor(mb1, mb1, mb2, ALU.add))
                settle()
                dve.tensor_copy(mb, mb1).then_inc(s.mask_ready, 1)
                dve.wait_ge(s.route_exp, rex.next())
                do(dve.reciprocal(r8[:, 6, :], r8[:, 1, :]))
                do(dve.tensor_scalar(r8[:, 7, :], r8[:, 5, :], 1.0, None, ALU.add))
                settle()
                do(dve.reciprocal(r8[:, 8, :], r8[:, 7, :]))
                settle()
                do(dve.tensor_tensor(gates[:, 0, :], r8[:, 6, :], r8[:, 8, :], ALU.mult))
                settle()
                do(dve.tensor_tensor(gates[:, 1, :], gates[:, 0, :], r8[:, 5, :], ALU.mult))
                do(dve.tensor_scalar(cols[:, 0:NE, :, 2], mb2.rearrange("p t e -> p e t"), float(SEQ), -float(OOB),
                                     ALU.mult, ALU.add))
                do(dve.memset(cols[:, NE:NE + 2, :, 2], 0.0))
                do(dve.tensor_copy(cols[:, :, :, 0], cst[:, K_TILE:K_TILE + NT].unsqueeze(1).broadcast_to([P, NE + 2, NT])))
                do(dve.tensor_copy(cols[:, :, :, 1], cst[:, K_P:K_P + 1].unsqueeze(2).broadcast_to([P, NE + 2, NT])))
                do(dve.memset(rank[:, NE:NE + 2, :], -1.0))
                dve.wait_ge(s.rank_full, rankf.next())
                do(dve.scalar_tensor_tensor(big, PS[:, 0:NT * NE].rearrange("p (t e) -> p t e", t=NT), 1.0, mb1,
                                            ALU.add, ALU.mult))
                settle()
                do(dve.tensor_scalar(rank[:, 0:NE, :].rearrange("p e t -> p t e"), big, -1.0, None, ALU.add))
                dve.tensor_reduce(nmax[:, :], PS[:, NT * NE:(NT + 1) * NE], AX.X, ALU.max).then_inc(s.nmax_ready, 1)
                settle()

            def onehot(e, r):
                dve.tensor_tensor(OH[:, r, :, :], iota[:, 0:CAP].unsqueeze(1).broadcast_to([P, NT, CAP]),
                                  bc(rank[:, e, :], CAP), ALU.is_equal).then_inc(s.onehot_ready, 1)

            def slot_ids(q, r):
                dve.wait_ge(s.ids_full, idf.next())
                do(dve.tensor_reduce(eids[0:CAP, q, 0:1], IDS[r][:, 0:2], AX.X, ALU.add))
                settle()
                dve.scalar_tensor_tensor(eids[0:CAP, q, 1:2], IDS[r][:, 2:3], float(OOB), eids[0:CAP, q, 0:1],
                                         ALU.add, ALU.add).then_inc(s.ids_ready, 1)

            def keep_rows():
                keep(gT[:, 4:8, :], PB[:, 0:4 * CAP].rearrange("p (k t) -> p k t", k=4))

            def phase3():
                route()
                dve.wait_ge(s.iota_loaded, iol.next())
                onehot(0, 0)
                onehot(1, 1)
                slot_ids(0, 0)
                slot_ids(1, 1)
                keep_rows()
                with n.loop(dve, "p3", 0, NE // 4) as j:
                    for q in range(4):
                        r = q % 2
                        onehot(j * 4 + (q + 2), r)
                        dve.wait_ge(s.silu_ready, silu.next())
                        dve.wait_ge(s.up_full, upf.next())
                        dve.tensor_tensor(hh[:, :, :], sg[:, :, :], UP, ALU.mult).then_inc(s.h_ready, 1)
                        dve.wait_ge(scattered[r], sct[r].last())
                        sct[r].next()
                        slot_ids((q + 2) % 4, r)
                        keep_rows()
                        dve.wait_ge(s.down_full, dn.next())
                        dve.tensor_copy(Y[0:CAP, r, HALF:D], DN[:, HALF:D]).then_inc(s.yb_ready, 1)

            def phase4():
                with n.loop(dve, "p4", 0, NT // 2) as j:
                    for r in range(2):
                        dve.wait_ge(cx_loaded[r], cxl[r].next(3))
                        for k in range(2):
                            dve.scalar_tensor_tensor(c_x[:, r, :], c_y[:, r, k, :], gates[:, k, bass.ds(j * 2 + r, 1)],
                                                     c_x[:, r, :], ALU.mult, ALU.add).then_inc(s.cx_ready, 1)
                            dve.wait_ge(s.cx_ready, cxr.next())

            dve.sem_inc(s.tb_free, 1)
            dve.sem_inc(s.yb_ready, 1)
            dve.wait_ge(s.consts_loaded, 32)
            dve.memset(put[:, :, :], 0.0).then_inc(s.consts_loaded, 1)
            dve.tensor_copy(tri[:, :], cst[:, K_TRI:K_TRI + P]).then_inc(s.consts_loaded, 1)
            dve.memset(ones[:, :], 1.0).then_inc(s.consts_loaded, 1)
            dve.memset(qout[MQ:P, HALF:2 * HALF], 0.0).then_inc(s.consts_loaded, 1)
            dve.wait_ge(s.consts_loaded, 36)
            with dve.Fori(0, DEPTH) as layer:
                n.enter_layer(layer)
                set_up_layer(layer)
                phase1()
                barrier(dve, phase)
                phase2()
                barrier(dve, phase)
                phase3()
                barrier(dve, phase)
                overflow_vector(dve, layer, layer + 1)
                phase4()
                barrier(dve, phase)
                n.leave_layer()

        @block.gpsimd
        def _(pool):
            n = Counts("pool")
            phase, step = n.on(s.phase_done, "phase"), n.on(s.step_pool, "step")
            var = n.on(s.var_ready, "var")
            inv, idr = n.on(s.inv_loaded, "inv", 16), n.on(s.ids_ready, "ids")
            ya, yb = n.on(s.ya_ready, "ya"), n.on(s.yb_ready, "yb")
            sct = [n.on(scattered[r], f"s{r}", 16) for r in range(2)]

            gth = [n.on(gathered[r], f"g{r}", 16) for r in range(2)]

            def rsqrt(c0, w):
                pool.wait_ge(s.var_ready, var.next())
                pool.tensor_tensor(st[:, 2, c0:c0 + w], st[:, 1, c0:c0 + w], cst[:, K_NH:K_NH + w],
                                   ALU.pow).then_inc(s.rstd_ready, 1)

            def do(ins):
                ins.then_inc(s.step_pool, 1)
                pool.wait_ge(s.step_pool, step.next())
                steady(pool)

            def pool_windows():
                lo, hi = slice(0, 64), slice(64, P)
                add = lambda o, a, b: do(pool.tensor_tensor(o, a, b, ALU.add))
                N = PAD + SEQ + PAD
                add(pool_a[:, :, 1:N], put[:, :, 0:N - 1], put[:, :, 1:N])
                add(pool_b[hi, 0, 2:N - 1], pool_a[hi, 0, 1:N - 2], pool_a[hi, 0, 3:N])
                add(pool_b[:, 1, 2:N - 1], pool_a[:, 1, 1:N - 2], pool_a[:, 1, 3:N])
                add(pool_a[:, 1, 4:N - 3], pool_b[:, 1, 2:N - 5], pool_b[:, 1, 6:N - 1])
                add(pool_b[hi, 1, 8:N - 7], pool_a[hi, 1, 4:N - 11], pool_a[hi, 1, 12:N - 3])
                pool.wait_ge(s.inv_loaded, inv.next(4))
                for c in range(2):
                    for part, buf in ((lo, pool_a), (hi, pool_b)):
                        w, u = buf[part, c, PAD:PAD + SEQ], put[part, c, PAD:PAD + SEQ]
                        do(pool.tensor_tensor(w, w, invc[part, c, :], ALU.mult))
                        do(pool.tensor_tensor(u, w, u, ALU.subtract))
                pool.sem_inc(s.pooled, 1)

            def phase1():
                rsqrt(20, 1)
                rsqrt(20, 1)
                rsqrt(0, NSTAT)

                def body(last):
                    rsqrt(0, 12)
                    if not last:
                        rsqrt(20, 1)
                    rsqrt(0, NSTAT)
                with n.loop(pool, "p1", 1, T):
                    body(False)
                body(True)
                rsqrt(0, 12)

            def phase2():
                def body(first, last):
                    for u in range(8):
                        if u == 0 and not first:
                            rsqrt(20, 1)
                        if u == 4:
                            rsqrt(12, 4)
                    if first:
                        pool_windows()
                body(True, False)
                with n.loop(pool, "p2", 1, T):
                    body(False, False)
                body(False, True)
                rsqrt(20, 1)

            def phase3():
                def gather(q, r):
                    pool.wait_ge(s.ids_ready, idr.next())
                    gather_rows(pool, q, r).then_inc(gathered[r], 16)
                    gth[r].next()
                gather(0, 0)
                gather(1, 1)
                with n.loop(pool, "p3", 0, NE // 4):
                    for q in range(4):
                        r = q % 2
                        gather((q + 2) % 4, r)
                        pool.wait_ge(s.ya_ready, ya.next() + 1)
                        pool.wait_ge(s.yb_ready, yb.next() + 1)
                        scatter_rows(pool, q, r).then_inc(scattered[r], 16)
                        sct[r].next()
                for r in range(2):
                    pool.wait_ge(scattered[r], sct[r].last())
                    pool.wait_ge(gathered[r], gth[r].last())

            pool.wait_ge(s.consts_loaded, 36)
            with pool.Fori(0, DEPTH) as layer:
                n.enter_layer(layer)
                phase1()
                barrier(pool, phase)
                phase2()
                barrier(pool, phase)
                phase3()
                barrier(pool, phase)
                overflow_gpsimd(pool, layer, layer + 1)
                barrier(pool, phase)
                n.leave_layer()

        @block.sync
        def _(sp):
            n = Counts("sp")
            phase = n.on(s.phase_done, "phase")
            xn, sr, bsd = n.on(s.xn_ready, "xn"), n.on(s.scores_ready, "sr"), n.on(s.biased, "biased")
            xup, hfr = n.on(s.x_updated, "xup"), n.on(s.hf_ready, "hf")
            xst, hst = n.on(s.x_stored, "xst", 16), n.on(s.h_stored, "hst", 16)
            pooled, dn = n.on(s.pooled, "pooled"), n.on(s.down_full, "dn")
            cxs = [n.on(cx_stored[r], f"cxs{r}", 16) for r in range(2)]

            def load_x(dst, i):
                sp.dma_start(dst, xs[tok(i), :]).then_inc(s.x_loaded, 16)

            def phase1(layer):
                load_x(xt1, 0)
                sp.dma_start(grow[:, :], gain_rows[layer, 0]).then_inc(s.gain_loaded, 16)
                for k in range(KD):
                    sp.dma_start(win[:, k, :], w_in[layer, k * P:(k + 1) * P, :]).then_inc(win_loaded[k], 16)
                with n.loop(sp, "p1", 1, NT) as i:
                    sp.wait_ge(s.xn_ready, xn.next())
                    steady(sp)
                    load_x(xt1, i)
                xn.next()

            def load_bias(i):
                sp.dma_start(bias, alibi[:, :, bass.ds((NT - 1 - i) * P, SEQ)]).then_inc(s.bias_loaded, 16)

            def phase2(layer):
                sp.dma_start(qs, q_dram[0]).then_inc(s.q_loaded, 16)
                load_bias(0)
                sp.dma_start(xt2, xs[0:P, :]).then_inc(s.x_loaded, 16)
                sp.dma_start(grow[:, :], gain_rows[layer, 1]).then_inc(s.gain_loaded, 16)
                sp.dma_start(wr[:, :, :], w_router[layer]).then_inc(s.wr_loaded, 16)
                for c in range(2):
                    for h, part in enumerate((slice(0, 64), slice(64, P))):
                        sp.dma_start(invc[part, c, :], inv_count[2 * c + h]).then_inc(s.inv_loaded, 16)
                sp.dma_start(wo, w_out[layer].rearrange("(k p) n -> p k n", p=P)).then_inc(s.wo_loaded, 16)

                def finish_h(i):
                    sp.wait_ge(s.hf_ready, hfr.next())
                    steady(sp)
                    sp.dma_start(h_dram[tok(i), :], hf).then_inc(s.h_stored, 16)
                    hst.next()

                def finish_x(i):
                    sp.wait_ge(s.x_updated, xup.next(2))
                    steady(sp)
                    sp.dma_start(xs[tok(i), :], xt2).then_inc(s.x_stored, 16)
                    xst.next()

                def body(i, first, last):
                    if not first:
                        finish_h(i - 1)
                        sp.wait_ge(s.x_stored, xst.last())
                        steady(sp)
                        load_x(xt2, i)
                    if not last:
                        sp.wait_ge(s.biased, bsd.next(8))
                        steady(sp)
                        load_bias(i + 1)
                        sp.wait_ge(s.scores_ready, sr.next(12))
                        steady(sp)
                        sp.dma_start(qs, q_dram[i + 1]).then_inc(s.q_loaded, 16)
                    finish_x(i)
                body(0, True, False)
                sp.wait_ge(s.pooled, pooled.next())
                steady(sp)
                load_expert(sp, layer, 0, 0, wload[0])
                with n.loop(sp, "p2", 1, T) as i:
                    body(i, False, False)
                body(T, False, True)
                finish_h(T)
                sp.wait_ge(s.x_stored, xst.last())
                steady(sp)
                sp.wait_ge(s.h_stored, hst.last())
                steady(sp)
                sr.next(12)
                bsd.next(8)

            def phase3(layer):
                sp.dma_start(iota, slots_iota).then_inc(s.iota_loaded, 16)
                for q in range(1, 4):
                    load_expert(sp, layer, q, q, wload[q])
                with n.loop(sp, "p3", 1, NE // 4) as j:
                    for q in range(4):
                        sp.wait_ge(s.down_full, dn.next())
                        steady(sp)
                        load_expert(sp, layer, j * 4 + q, q, wload[q])
                dn.next(4)

            def phase4():
                with n.loop(sp, "p4", 0, NT // 2) as j:
                    for r in range(2):
                        i = j * 2 + r
                        sp.wait_ge(cx_stored[r], cxs[r].last())
                        steady(sp)
                        cxs[r].next()
                        sp.dma_start(c_x[:, r, :], xs[tok(i), :]).then_inc(cx_loaded[r], 16)
                        for k in range(2):
                            sp.dma_start(c_y[:, r, k, :], y_dram[bass.ds(k * SEQ + i * P, P), :]).then_inc(cx_loaded[r], 16)

            sp.dma_start(cst[:, :], consts).then_inc(s.consts_loaded, 16)
            sp.dma_start(sm[:, :, :], small).then_inc(s.consts_loaded, 16)
            sp.dma_start(xs[:, :], x[0]).then_inc(s.x_copied, 16)
            sp.wait_ge(s.x_copied, 16)
            with sp.Fori(0, DEPTH) as layer:
                n.enter_layer(layer)
                sp.dma_start(wuq[:, 0, :], w_uq[layer, 0:P, :]).then_inc(s.weights_loaded, 16)
                sp.dma_start(wuq[0:QR - P, 1, :], w_uq[layer, P:QR, :]).then_inc(s.weights_loaded, 16)
                sp.dma_start(wukv[:, :], w_ukv[layer]).then_inc(s.weights_loaded, 16)
                sp.dma_start(pwd[:, :, :], pool_w[layer]).then_inc(s.weights_loaded, 16)
                phase1(layer)
                barrier(sp, phase)
                phase2(layer)
                barrier(sp, phase)
                phase3(layer)
                barrier(sp, phase)
                overflow_sync(sp, layer, layer + 1)
                phase4()
                barrier(sp, phase)
                n.leave_layer()


def kernel(x, norm1_g, w_in, diff_q_norm_g, diff_k_norm_g, diff_lambda, diff_sub_norm_g,
           mla_q_lat_norm_g, mla_kv_lat_norm_g, mla_w_uq, mla_w_ukv,
           mla_q_nope_norm_g, mla_q_rope_norm_g, mla_k_nope_norm_g, mla_k_rope_norm_g,
           pool_w, pool_scale, w_out, norm2_g,
           router_group_w, router_group_b, router_expert_w, router_expert_b,
           expert_w_gate, expert_w_up, expert_w_down):
    import numpy as np
    import concourse.bacc as bacc
    from concourse.bass_utils import run_bass_kernel_spmd

    f = np.float32
    L_ = DEPTH
    small = np.zeros((P, L_, N_SM), f)
    rows = lambda a: np.broadcast_to(np.asarray(a)[None], (P,) + np.asarray(a).shape)
    for h in range(2):
        small[h * 64:h * 64 + 64, :, C_DQG] = np.asarray(diff_q_norm_g).T
        small[h * 64:h * 64 + 64, :, C_DKG] = np.asarray(diff_k_norm_g).T
    small[:, :, C_SUB] = np.asarray(diff_sub_norm_g).T
    small[:, :, C_QL] = np.asarray(mla_q_lat_norm_g)[:, 0:P].T
    small[0:QR - P, :, C_QL + 1] = np.asarray(mla_q_lat_norm_g)[:, P:QR].T
    small[:, :, C_KVL] = np.asarray(mla_kv_lat_norm_g).T
    small[0:NOPE, :, C_MQG] = np.asarray(mla_q_nope_norm_g).T
    small[NOPE:MQ, :, C_MQG] = 1.0
    small[0:NOPE, :, C_MKG] = np.asarray(mla_k_nope_norm_g).T
    small[NOPE:MQ, :, C_MKG] = 1.0
    for c in range(2):
        small[:, :, C_PS + c] = np.asarray(pool_scale)[:, c * P:(c + 1) * P].T
    for c, g in ((C_RGQ, mla_q_rope_norm_g), (C_RGK, mla_k_rope_norm_g)):
        g = np.asarray(g)
        small[:, :, c:c + ROPE] = rows(g)
        small[:, :, c + ROPE:c + ROPE + 16] = rows(g[:, 16:32])
        small[:, :, c + ROPE + 16:c + 2 * ROPE] = rows(g[:, 0:16])
    small[:, :, C_RB:C_RB + NG] = rows(router_group_b)
    small[:, :, C_RB + NG:C_RB + NLOG] = rows(router_expert_b)
    small[:, :, C_LAM:C_LAM + 4 * DQ] = rows(np.asarray(diff_lambda).reshape(L_, 4 * DQ))
    for layer in range(L_):
        lam_init = 0.8 - 0.6 * math.exp(-0.3 * layer)
        small[:, layer, C_LI] = lam_init
        small[:, layer, C_LI + 1] = 1.0 - lam_init
    gain_rows = np.ascontiguousarray(np.broadcast_to(
        np.stack([np.asarray(norm1_g), np.asarray(norm2_g)], axis=1)[:, :, None, :], (L_, 2, P, D)))
    pw = np.zeros((L_, P, 2, P), f)
    for g in range(4):
        h = 64 * (g % 2)
        pw[:, h:h + 64, g // 2, h:h + 64] = np.asarray(pool_w)[:, g]
    wr = np.ascontiguousarray(np.concatenate([np.asarray(router_group_w), np.asarray(router_expert_w)], axis=2)
                              .reshape(L_, KD, P, NLOG).transpose(0, 2, 1, 3))
    cst = np.zeros((P, N_K), f)
    cst[:, K_ID:K_ID + P] = np.eye(P)
    inv = (1.0 / (10000.0 ** (np.arange(0, ROPE, 2, dtype=f) / ROPE))).astype(f)
    ang = (np.arange(SEQ, dtype=f)[:, None] * inv[None, :]).astype(f)
    for k, a in ((K_COS, (np.cos(ang), np.cos(ang))), (K_SIN, (-np.sin(ang), np.sin(ang)))):
        t = np.concatenate(a, axis=1).astype(f).reshape(NT, P, ROPE).transpose(1, 0, 2)
        cst[:, k:k + NT * ROPE] = t.reshape(P, NT * ROPE)
    cst[:, K_INV:K_INV + NSTAT] = [1 / DQ] * 16 + [1 / QR, 1 / KVR, 1 / ROPE]
    cst[:, K_INV2:K_INV2 + 12] = [1 / NOPE] * 4 + [1 / ROPE] * 4 + [1 / NOPE] * 4
    cst[:, K_I8:K_I8 + 8] = np.arange(8)
    cst[:, K_TILE:K_TILE + NT] = np.arange(NT) * P
    cst[:, K_P] = np.arange(P)
    cst[:, K_TRI:K_TRI + P] = np.triu(np.ones((P, P)), 1)
    cst[:, K_NH:] = -0.5
    dist = np.abs(np.arange(P)[:, None] - np.arange(1920)[None, :] + (SEQ - P))
    alibi = np.stack([dist * 2.0 ** (-8.0 * (h + 1) / DH) for h in range(DH)], axis=1).astype(np.float16)
    t = np.arange(SEQ)
    count = [np.minimum(t + w // 2 - 1, SEQ - 1) - np.maximum(t - w // 2, 0) + 1 for w in WINDOWS]
    inv_count = np.ascontiguousarray(np.broadcast_to(np.stack([(1.0 / c).astype(f) for c in count])[:, None], (4, 64, SEQ)))
    iota = np.ascontiguousarray(np.broadcast_to(np.arange(SEQ + CAP, dtype=f), (P, SEQ + CAP)))

    nc = bacc.Bacc("TRN2", target_bir_lowering=False, num_devices=1)
    arrays, args = {}, []
    for name, a in (("x", x), ("w_in", w_in), ("w_uq", mla_w_uq), ("w_ukv", mla_w_ukv), ("pool_w", pw),
                    ("w_out", w_out), ("w_router", wr), ("w_gate", expert_w_gate), ("w_up", expert_w_up),
                    ("w_down", expert_w_down), ("small", small), ("gain_rows", gain_rows), ("consts", cst),
                    ("alibi", alibi), ("inv_count", inv_count), ("iota", iota)):
        a = np.ascontiguousarray(a)
        arrays[f"in_{name}"] = a
        args.append(nc.dram_tensor(f"in_{name}", a.shape, mybir.dt.from_np(a.dtype), kind="ExternalInput").ap())
    out = nc.dram_tensor("out_0", (1, SEQ, D), F32, kind="ExternalOutput").ap()
    program(nc, *args, out)
    r = run_bass_kernel_spmd(nc, [arrays], core_ids=[0])
    return r.results[0]["out_0"]
```

```python
import math
from collections import namedtuple
from contextlib import ExitStack, contextmanager

import concourse.bass as bass
from concourse import mybir

F32 = mybir.dt.float32
F16 = mybir.dt.float16
BF16 = mybir.dt.bfloat16
I32 = mybir.dt.int32
U32 = mybir.dt.uint32
ALU = mybir.AluOpType
ACT = mybir.ActivationFunctionType
AX = mybir.AxisListType

P = 128
SEQ = 1024
D = 1024
DEPTH = 2
NT = SEQ // P
KD = D // P
HALF = 512
DH = 4
DV = 128
DQ = 64
MH = 4
NOPE, ROPE, MV = 64, 32, 64
MQ = NOPE + ROPE
QR, KVR = 192, 128
PW = 256
WINDOWS = (2, 4, 8, 16)
PAD = 8
D_IN = 2144
O_LAT = 1024
O_KR = O_LAT + QR + KVR
O_PU = O_KR + ROPE
PJ = O_PU + PW
ORDER = (0, 4, 3, 1, 2)
CHUNKS = ((0, 512), (512, 512), (1024, 512), (1536, 352), (1888, 256))
NG, EPG = 4, 8
NE = NG * EPG
FF = 256
CAP = 96
OVER = -(-SEQ // CAP) - 1
SLOT = 2 * KD * FF + 2 * D
EPS = 1e-6
NLOG = NG + NE
OOB = 4096
DONE = 16
NSTAT = 19

C_DQG, C_DKG, C_SUB, C_QL, C_KVL, C_MQG, C_MKG, C_PS = 0, 1, 2, 3, 5, 6, 7, 8
C_RGQ, C_RSQ, C_RGK, C_RSK = 10, 42, 74, 106
C_RB = 138
C_LAM = C_RB + NLOG
C_LI = C_LAM + 4 * DQ
N_SM = C_LI + 2
K_ID, K_COS, K_SIN, K_INV, K_INV2, K_I8, K_TILE, K_P, K_TRI, K_NH = 0, 128, 384, 640, 659, 671, 679, 687, 688, 816
N_K = K_NH + 24


class Count:

    def __init__(self, sem, per_layer, unit=1, credit=0):
        self.sem, self.per_layer, self.unit, self.credit = sem, per_layer, unit, credit
        self.k = 0
        self.layer = self.step = None
        self.per_step = 0

    def value(self, k):
        v = self.layer * (self.per_layer * self.unit) if self.layer is not None else 0
        if self.step is not None and self.per_step:
            v = v + self.step * (self.per_step * self.unit)
        return v + (k * self.unit + self.credit)

    def next(self, n=1):
        self.k += n
        return self.value(self.k)

    def last(self):
        return self.value(self.k)


class Counts:

    def __init__(self, name):
        self.name, self.all = name, {}
        self.table, self.loops = USES.get(name, {}), LOOP_USES.get(name, {})
        self.seen, self.seen_loops = {}, {}

    def on(self, sem, key, unit=1, credit=0):
        c = self.all[key] = Count(sem, self.table.get(key, 0), unit, credit)
        return c

    def enter_layer(self, layer):
        for c in self.all.values():
            c.layer, c.k = layer, 0

    def leave_layer(self):
        self.seen = {key: c.k for key, c in self.all.items() if c.k}
        if self.seen != self.table or self.seen_loops != self.loops:
            raise ValueError(f"uses of {self.name}: {self.seen}, {self.seen_loops}")

    @contextmanager
    def loop(self, eng, key, first, end, by=1):
        per_step = self.loops.get(key, {})
        with eng.Fori(first, end) as step:
            start = {}
            for k, c in self.all.items():
                c.per_step = per_step.get(k, 0)
                c.step, start[k] = step, c.k
                c.k -= c.per_step * first
            yield step
        self.seen_loops[key] = {}
        for k, c in self.all.items():
            used = c.k + c.per_step * first - start[k]
            if used:
                self.seen_loops[key][k] = used
            c.k = start[k] + used * (end - first)
            c.step, c.per_step = None, 0


USES = {'act': {'phase': 20,
         'ta': 153,
         'mine': 153,
         'x': 8,
         'pf': 40,
         'qst': 8,
         'biased': 64,
         'max': 32,
         'xup': 16,
         'rarg': 2,
         'lam': 1,
         'gf': 32,
         'dn': 32,
         'yf': 32,
         'small': 1},
 'dve': {'phase': 20,
         'step': 405,
         'tb': 169,
         'mine': 169,
         'xsq': 16,
         'rstd': 40,
         'kept': 40,
         'gl': 2,
         'bl': 8,
         'lamx': 1,
         'sr': 96,
         'exp': 96,
         'pv': 64,
         'x': 8,
         'x2': 8,
         'hst': 8,
         'cur': 1,
         'iota': 1,
         'rex': 2,
         'rank': 1,
         'ids': 34,
         'silu': 32,
         'up': 32,
         'dn': 32,
         'yf': 32,
         'out': 16,
         'small': 1},
 'pe': {'phase': 20,
        'ta': 153,
        'tb': 169,
        'xn': 8,
        'kept': 40,
        'pjn': 8,
        'mln': 8,
        'win': 1,
        'ql': 8,
        'wo': 1,
        'biased': 64,
        'exp': 96,
        'mixed': 32,
        'xup': 16,
        'od': 8,
        'om': 8,
        'pooled': 1,
        'hf': 8,
        'mask': 1,
        'oh': 34,
        'g0': 17,
        'g1': 17,
        'w0': 24,
        'w1': 24,
        'w2': 24,
        'w3': 21,
        'w4': 3,
        'h': 32,
        'ya': 32,
        'yb': 32,
        'wr': 1,
        'wt': 4},
 'pool': {'phase': 20,
          'step': 13,
          'var': 40,
          'inv': 4,
          'ids': 34,
          'ya': 32,
          'yb': 32,
          's0': 16,
          's1': 16,
          'g0': 17,
          'g1': 17},
 'sp': {'phase': 20,
        'xn': 8,
        'sr': 96,
        'biased': 64,
        'xup': 16,
        'hf': 8,
        'xst': 16,
        'hst': 8,
        'pooled': 1,
        'dn': 32,
        'xc': 8,
        'pv': 64,
        'g1': 17,
        'qst': 8,
        'kept': 40}}
LOOP_USES = {'act': {'p1': {'ta': 8, 'mine': 8, 'x': 2, 'pf': 10, 'qst': 2},
         'p2': {'ta': 22, 'mine': 22, 'biased': 16, 'max': 8, 'xup': 4},
         'p3': {'ta': 4, 'mine': 4, 'gf': 4, 'dn': 4, 'yf': 4}},
 'dve': {'p1': {'step': 52, 'tb': 12, 'mine': 12, 'xsq': 2, 'rstd': 6, 'kept': 10, 'x': 2},
         'p2': {'step': 30,
                'tb': 22,
                'mine': 22,
                'xsq': 2,
                'rstd': 4,
                'bl': 2,
                'sr': 24,
                'exp': 24,
                'pv': 16,
                'x2': 2,
                'hst': 2,
                'out': 4},
         'p3': {'step': 4, 'tb': 4, 'mine': 4, 'ids': 4, 'silu': 4, 'up': 4, 'dn': 4, 'yf': 4}},
 'pe': {'p1': {'ta': 8, 'tb': 12, 'xn': 2, 'kept': 10, 'pjn': 2, 'mln': 2},
        'p2': {'ta': 22, 'tb': 22, 'ql': 2, 'biased': 16, 'exp': 24, 'mixed': 8, 'xup': 4, 'od': 2, 'om': 2, 'hf': 2},
        'p3': {'ta': 4,
               'tb': 4,
               'oh': 4,
               'g0': 2,
               'g1': 2,
               'w0': 3,
               'w1': 3,
               'w2': 3,
               'w3': 3,
               'h': 4,
               'ya': 4,
               'yb': 4}},
 'pool': {'p1': {'var': 6}, 'p2': {'var': 2}, 'p3': {'ids': 4, 'ya': 4, 'yb': 4, 's0': 2, 's1': 2, 'g0': 2, 'g1': 2}},
 'sp': {'p1': {'xn': 1, 'xst': 1, 'xc': 1},
        'p2': {'sr': 24, 'biased': 16, 'xup': 4, 'hf': 2, 'xst': 2, 'hst': 2, 'pv': 16},
        'p3': {'dn': 4}}}


def program(nc, x, w_in, w_uq, w_ukv, pool_w, w_out, w_router, w_gate, w_up, w_down,
            small, gain_rows, consts, alibi, inv_count, slots_iota, out):
    dram = lambda name, shape: nc.dram_tensor(name, shape, F32, kind="Internal").ap()
    q_dram = dram("q_dram", [NT, P, 2 * HALF])
    h_dram = dram("h_dram", [SEQ, D])
    y_dram = dram("y_dram", [2 * SEQ, D])
    xs = out[0]

    ctx = ExitStack()
    with ctx, nc.allow_low_precision(reason="whole numbers below 2**24 become indices"):
        sb = lambda name, shape, dt=F32: ctx.enter_context(nc.sbuf_tensor(name, shape, dt))
        sem = lambda name: ctx.enter_context(nc.semaphore(name))

        cur = sb("cur", [P, N_SM])
        der = sb("der", [P, 16])
        cst = sb("cst", [P, N_K])
        grow = sb("grow", [P, D])
        put = sb("put", [P, 2, PAD + SEQ + PAD])
        tri = sb("tri", [P, P], BF16)
        ones = sb("ones", [P, P], BF16)
        logits = sb("logits", [P, NT, NLOG])
        gates = sb("gates", [P, 2, NT])
        nmax = sb("nmax", [P, 1], I32)
        st = sb("st", [P, 3, 24])
        pwd = sb("pwd", [P, 2, P])
        wreg = sb("wreg", [P, 3 * SLOT])
        qreg = sb("qreg", [P, 14336])
        WORK = 13760
        work = sb("work", [P, WORK])

        def flat(region, start, shape):
            n = math.prod(shape)
            assert start + n <= region.shape[1], (start, shape)
            a = region[:, start:start + n]
            if len(shape) == 2:
                a = a.rearrange("p (a b) -> p a b", b=shape[1])
            if len(shape) == 3:
                a = a.rearrange("p (a b c) -> p a b c", b=shape[1], c=shape[2])
            return a

        class Lay:
            def __init__(self, region, at=0):
                self.region, self.at = region, at

            def take(self, *shape):
                a = flat(self.region, self.at, shape)
                self.at += math.prod(shape)
                return a

        L = Lay(qreg)
        kT = L.take(DH, SEQ)
        kmT = L.take(MH, SEQ)
        V = L.take(NT, DH * DV)
        VM = L.take(NT, MH * MV)
        win = flat(wreg, 0, (KD, D_IN))
        L = Lay(work)
        xt1, xn1 = L.take(D), L.take(D)
        yt1 = L.take(2, D)
        hT1 = [L.take(KD, P), flat(wreg, KD * D_IN, (KD, P))]
        pj = L.take(PJ)
        sq = L.take(O_PU)
        mj = L.take(MH * MQ + MH * P)
        qc, kc = L.take(MH, MQ), L.take(MH, MQ)
        latT = L.take(3, P)
        rt, rt2 = L.take(MH, ROPE), L.take(MH, ROPE)
        qout = L.take(2 * HALF)
        wuq, wukv = L.take(2, MH * MQ), L.take(MH * P)
        rope = L.take(4 * NT, ROPE).rearrange("p (a t) r -> p a t r", a=4)
        pool_a, pool_b = flat(wreg, 0, (2, PAD + SEQ + PAD)), flat(wreg, 2 * 1040, (2, PAD + SEQ + PAD))
        invc = flat(wreg, 4 * 1040, (2, SEQ))
        wo = flat(wreg, 6400, (KD, D))
        bias = wreg[:, 6400 + KD * D:6400 + KD * D + DH * SEQ // 2].bitcast(F16).rearrange("p (h j) -> p h j", h=DH)
        L = Lay(work)
        qs = [L.take(2 * HALF), flat(wreg, 16640, (2 * HALF,))]
        SC = L.take(2, SEQ)
        E = L.take(4, SEQ)
        AT = L.take(NT, P)
        ob = L.take(DH * DV)
        om = L.take(MH * MV)
        osq = L.take(DH * DV)
        catT = L.take(KD, P)
        xt2 = L.take(D)
        hf = L.take(D)
        hT2 = catT
        junk2 = L.take(D)
        assert L.at <= WORK, L.at
        wr = sb("wr", [P, KD, NLOG])
        rs, rc, mn = sb("rs", [P, 12]), sb("rc", [P, 12]), sb("mn", [P, 12])
        cf = sb("cf", [P, DH])
        slot = [wreg[:, 0:SLOT], wreg[:, SLOT:2 * SLOT], qreg[:, 0:SLOT], qreg[:, SLOT:2 * SLOT],
                wreg[:, 2 * SLOT:3 * SLOT]]
        L = Lay(work)
        G = L.take(2, D)
        gT = L.take(KD, CAP)
        sg, hh = L.take(2, CAP), L.take(2, CAP)
        Y = L.take(2, D)
        iota = L.take(SEQ + CAP)
        rank = L.take(NE + 2, NT)
        mb1, mb2 = L.take(NT, NE), L.take(NT, NE)
        big = L.take(NT, NE)
        gm_, ge_, gv_, gk_ = L.take(NT, NG), L.take(NT, NG), L.take(NT, NG), L.take(NT, NG)
        es, ev, ek1, ek2 = L.take(NT, EPG), L.take(NT, EPG), L.take(NT, EPG), L.take(NT, EPG)
        r8 = L.take(16, NT)
        eids = L.take(4, 2).bitcast(U32)
        OH = work[:, L.at:L.at + NT * CAP].bitcast(BF16).rearrange("p (r t s) -> p r t s", r=2, t=NT)
        L.at += NT * CAP
        n = (NE + 2) * NT * 3 // 2
        cols = work[:, L.at:L.at + n].bitcast(BF16).rearrange("p (e t c) -> p e t c", e=NE + 2, t=NT)
        L.at += n
        mb = work[:, L.at:L.at + P].bitcast(BF16).rearrange("p (t e) -> p t e", t=NT)
        L.at += P
        assert L.at <= WORK, L.at
        c_x = [flat(wreg, i * D, (D,)) for i in range(NT)]
        RING = 6
        c_y = flat(work, 0, (RING * 2, D))

        PA = ctx.enter_context(nc.psum_tensor("PA", [P, HALF], F32))
        PB = ctx.enter_context(nc.psum_tensor("PB", [P, HALF], F32))
        PS = ctx.enter_context(nc.psum_tensor("PS", [P, 6 * HALF], F32))
        S = [PS[:, 0:SEQ], PS[:, SEQ:2 * SEQ]]
        OD = PS[:, 2 * SEQ:2 * SEQ + HALF].rearrange("p (h e) -> p h e", h=DH)
        OUT = [PS[:, 2 * SEQ + h * HALF:2 * SEQ + (h + 1) * HALF] for h in range(2)]
        OM = PS[:, 2 * SEQ + HALF:2 * SEQ + HALF + MH * MV].rearrange("p (h e) -> p h e", h=MH)
        GATE, UP = (PS[:, b * HALF:b * HALF + 2 * CAP].rearrange("p (f s) -> p f s", f=2) for b in range(2))
        DN = PS[0:CAP, SEQ:2 * SEQ]
        IDS = [PS[0:CAP, (4 + r) * HALF:(4 + r) * HALF + 3] for r in range(2)]

        ident = cst[:, K_ID:K_ID + P]
        NQS, NSUB, NLAM, MQS, X1 = 0, 1, 2, 3, 4

        names = [
            "phase_done", "carried", "consts_loaded", "small_ready", "lam_exp", "lam_sum", "step_dve", "step_pool",
            "win_loaded0", "x_loaded", "gain_loaded", "x_squared", "var_ready", "rstd_ready", "xn_ready",
            "ta_full", "ta_free", "tb_full", "tb_free", "proj_full", "proj_kept", "pj_normed", "mla_normed",
            "q_stored", "q_loaded", "bias_loaded", "wo_loaded", "x_stored", "h_stored",
            "scores_ready", "biased", "max_ready", "exp_done", "mixed", "pv_done",
            "od_ready", "om_ready", "pooled", "inv_loaded", "x_updated", "out_full", "hf_ready",
            "iota_loaded", "wr_loaded", "weights_loaded", "route_exp", "route_arg", "mask_ready", "rank_full", "nmax_ready",
            "onehot_ready", "ids_full", "ids_ready", "gathered0", "gathered1", "gate_full", "up_full", "silu_ready",
            "h_ready", "down_full", "y_free", "ya_ready", "yb_ready", "scattered0", "scattered1",
            "w0_loaded", "w1_loaded", "w2_loaded", "w3_loaded", "w4_loaded",
            "x_combined", "x2_loaded", "cur_loaded", "held_loaded", "cy_loaded", "cx_half", "cx_ready", "cx_stored",
            "o_w", "o_onehot", "o_ids", "o_conv", "o_g", "o_t", "o_ev", "o_gu", "o_silu", "o_h", "o_dn", "o_y",
            "o_s", "o_free"]
        s = namedtuple("Semaphores", names)(*[sem(name) for name in names])
        wload = [s.w0_loaded, s.w1_loaded, s.w2_loaded, s.w3_loaded, s.w4_loaded]
        gathered, scattered = [s.gathered0, s.gathered1], [s.scattered0, s.scattered1]
        cy_loaded = [s.cy_loaded] + [sem(f"cy_loaded{r}") for r in range(1, RING)]
        win_loaded = [s.win_loaded0] + [sem(f"win_loaded{k}") for k in range(1, KD)]

        T = NT - 1

        def maps(u, only=None):
            both = (2 * u, 2 * u + 1) if u < DH else (u + 4,)
            return both if only is None else both[only:only + 1]

        tok = lambda i: bass.ds(i * P, P)
        block = ctx.enter_context(nc.Block())

        def steady(eng):
            eng.sem_inc(s.carried, 1)

        def barrier(eng, phase):
            steady(eng)
            eng.drain().then_inc(s.phase_done, 1)
            eng.wait_ge(s.phase_done, phase.next(5))
            steady(eng)

        NB = NE * OVER

        @contextmanager
        def further_blocks(eng, layer, load_ready, raised):
            eng.wait_ge(s.nmax_ready, load_ready)
            steady(eng)
            most = eng.value_load(nmax[0:1, 0:1], min_val=0, max_val=SEQ)
            with eng.If(most > CAP):
                with eng.Fori(0, NE) as e:
                    with eng.Fori(0, OVER) as c:
                        yield e, c, layer * NB + e * OVER + c
            with eng.Else():
                for which, by in raised:
                    eng.sem_inc(which, NB * by)

        def overflow_tensor(pe, layer, ready, up_matmuls, down_matmuls):
            with further_blocks(pe, layer, ready, ((s.o_ids, 1), (s.o_t, 1), (s.o_gu, 1), (s.o_dn, 1))) as (e, c, b):
                pe.wait_ge(s.o_onehot, b + 1)
                for i in range(NT):
                    t = pe.matmul(IDS[0], OH[:, 0, i, :], cols[:, e, i, :], start=(i == 0), stop=(i == NT - 1))
                t.then_inc(s.o_ids, 1)
                pe.wait_ge(s.o_g, (b + 1) * 16)
                for bank, k0 in ((PA, 0), (PB, 4)):
                    for k in range(4):
                        t = pe.transpose(bank[:, k * CAP:(k + 1) * CAP],
                                         G[0:CAP, 0, k0 + k:D:KD], ident[0:CAP, 0:CAP])
                t.then_inc(s.o_t, 1)
                pe.wait_ge(s.o_ev, b * 2 + 2)
                pe.wait_ge(s.o_w, (b + 1) * 48)
                up_matmuls(slot[3][:, 0:KD * FF], GATE)
                up_matmuls(slot[3][:, KD * FF:2 * KD * FF], UP).then_inc(s.o_gu, 1)
                pe.wait_ge(s.o_h, b + 1)
                down_matmuls(slot[3][:, 2 * KD * FF:]).then_inc(s.o_dn, 1)

        def overflow_scalar(act, layer, ready):
            with further_blocks(act, layer, ready, ((s.o_silu, 1),)) as (e, c, b):
                act.wait_ge(s.o_gu, b + 1)
                act.activation(sg[:, :, :], GATE, ACT.Silu).then_inc(s.o_silu, 1)

        def overflow_vector(dve, layer, ready):
            raised = ((s.o_onehot, 1), (s.o_conv, 2), (s.o_ev, 2), (s.o_h, 1), (s.o_y, 2))
            with further_blocks(dve, layer, ready, raised) as (e, c, b):
                dve.tensor_tensor(OH[:, 0, :, :], iota[:, bass.ds((c + 1) * CAP, CAP)].unsqueeze(1).broadcast_to([P, NT, CAP]),
                                  rank[:, e, :].unsqueeze(2).broadcast_to([P, NT, CAP]),
                                  ALU.is_equal).then_inc(s.o_onehot, 1)
                dve.wait_ge(s.o_ids, b + 1)
                dve.wait_ge(s.o_free, b + 1)
                dve.tensor_reduce(eids[0:CAP, 0, 0:1], IDS[0][:, 0:2], AX.X, ALU.add).then_inc(s.o_conv, 1)
                dve.wait_ge(s.o_conv, b * 2 + 1)
                dve.scalar_tensor_tensor(eids[0:CAP, 0, 1:2], IDS[0][:, 2:3], float(OOB), eids[0:CAP, 0, 0:1],
                                         ALU.add, ALU.add).then_inc(s.o_conv, 1)
                dve.wait_ge(s.o_t, b + 1)
                dve.tensor_copy(gT[:, 0:4, :], PA[:, 0:4 * CAP].rearrange("p (k s) -> p k s", k=4)).then_inc(s.o_ev, 1)
                dve.tensor_copy(gT[:, 4:8, :], PB[:, 0:4 * CAP].rearrange("p (k s) -> p k s", k=4)).then_inc(s.o_ev, 1)
                dve.wait_ge(s.o_silu, b + 1)
                dve.tensor_tensor(hh[:, :, :], sg[:, :, :], UP, ALU.mult).then_inc(s.o_h, 1)
                dve.wait_ge(s.o_dn, b + 1)
                for half in range(2):
                    dve.tensor_copy(Y[0:CAP, 0, half * HALF:(half + 1) * HALF],
                                    DN[:, half * HALF:(half + 1) * HALF]).then_inc(s.o_y, 1)

        def overflow_gpsimd(pool, layer, ready):
            with further_blocks(pool, layer, ready, ((s.o_g, 16), (s.o_s, 16), (s.o_free, 1))) as (e, c, b):
                pool.wait_ge(s.o_conv, b * 2 + 2)
                gather_rows(pool, 0, 0).then_inc(s.o_g, 16)
                pool.wait_ge(s.o_y, b * 2 + 2)
                scatter_rows(pool, 0, 0).then_inc(s.o_s, 16)
                pool.wait_ge(s.o_s, (b + 1) * 16)
                pool.sem_inc(s.o_free, 1)

        def overflow_sync(sp, layer, ready):
            with further_blocks(sp, layer, ready, ((s.o_w, 48),)) as (e, c, b):
                sp.wait_ge(s.o_free, b + 1)
                steady(sp)
                load_expert(sp, layer, e, 3, s.o_w)
            with sp.If(sp.value_load(nmax[0:1, 0:1], min_val=0, max_val=SEQ) > CAP):
                sp.wait_ge(s.o_free, (layer + 1) * NB + 1)
                steady(sp)

        def load_expert(sp, layer, e, q, landed):
            w = slot[q]
            for src, at, k in ((w_gate, 0, KD), (w_up, KD * FF, KD), (w_down, 2 * KD * FF, 2)):
                n = FF if k == KD else D
                sp.dma_start(w[:, at:at + k * n].rearrange("p (k n) -> p k n", k=k),
                             src[layer, e].rearrange("(p k) n -> p k n" if k == KD else "(k p) n -> p k n", p=P)
                             ).then_inc(landed, 16)

        def gather_rows(pool, q, r):
            steady(pool)
            return pool.indirect_dma_start(out=G[0:CAP, r, :], out_offset=None, in_=h_dram[:, :],
                                           in_offset=bass.IndirectOffsetOnAxis(ap=eids[0:CAP, q, 0:1], axis=0),
                                           bounds_check=SEQ - 1, oob_is_err=False)

        def scatter_rows(pool, q, r):
            steady(pool)
            return pool.indirect_dma_start(out=y_dram[:, :],
                                           out_offset=bass.IndirectOffsetOnAxis(ap=eids[0:CAP, q, 1:2], axis=0),
                                           in_=Y[0:CAP, r, :], in_offset=None,
                                           bounds_check=2 * SEQ - 1, oob_is_err=False)

        @block.tensor
        def _(pe):
            n = Counts("pe")
            phase = n.on(s.phase_done, "phase")
            ta, tb = n.on(s.ta_free, "ta"), n.on(s.tb_free, "tb")
            xn, kept = n.on(s.xn_ready, "xn"), n.on(s.proj_kept, "kept")
            pjn, mln = n.on(s.pj_normed, "pjn"), n.on(s.mla_normed, "mln")
            win_c = n.on(s.win_loaded0, "win", 16)
            ql, wol = n.on(s.q_loaded, "ql", 16), n.on(s.wo_loaded, "wo", 16)
            biased, expd = n.on(s.biased, "biased"), n.on(s.exp_done, "exp")
            mixed, xup, odr, omr = n.on(s.mixed, "mixed"), n.on(s.x_updated, "xup"), n.on(s.od_ready, "od"), n.on(s.om_ready, "om")
            pooled, hfr = n.on(s.pooled, "pooled"), n.on(s.hf_ready, "hf")
            masks, oh, gth = n.on(s.mask_ready, "mask"), n.on(s.onehot_ready, "oh"), [
                n.on(gathered[r], f"g{r}", 16) for r in range(2)]
            wl = [n.on(wload[r], f"w{r}", 16) for r in range(5)]
            hr, ya, yb = n.on(s.h_ready, "h"), n.on(s.ya_ready, "ya"), n.on(s.yb_ready, "yb")
            wrl, wtl = n.on(s.wr_loaded, "wr", 16), n.on(s.weights_loaded, "wt", 16)

            def evacuated(c):
                pe.wait_ge(c.sem, c.value(c.k + 1))

            def turn_x():
                pe.wait_ge(s.xn_ready, xn.next())
                for c, bank, full, k0 in ((tb, PB, s.tb_full, 4), (ta, PA, s.ta_full, 0)):
                    pe.wait_ge(c.sem, c.next())
                    for k in range(4):
                        t = pe.transpose(bank[:, k * P:(k + 1) * P], xn1[:, (k0 + k) * P:(k0 + k + 1) * P], ident)
                    t.then_inc(full, 1)

            def project(c, odd):
                c0, w = CHUNKS[c]
                pe.wait_ge(s.proj_kept, kept.next())
                for k in range(KD):
                    t = pe.matmul(PS[:, c * HALF:c * HALF + w], hT1[odd][:, k, :], win[:, k, c0:c0 + w],
                                  start=(k == 0), stop=(k == KD - 1))
                t.then_inc(s.proj_full, 1)

            def project_first():
                win_c.next()
                for k in range(KD):
                    pe.wait_ge(win_loaded[k], win_c.last())
                    for c in ORDER:
                        c0, w = CHUNKS[c]
                        t = pe.matmul(PS[:, c * HALF:c * HALF + w], hT1[0][:, k, :], win[:, k, c0:c0 + w],
                                      start=(k == 0), stop=(k == KD - 1))
                        if k == KD - 1:
                            t.then_inc(s.proj_full, 1)

            def turn_maps():
                pe.wait_ge(s.pj_normed, pjn.next())
                for c, bank, full, c0 in ((ta, PA, s.ta_full, 0), (tb, PB, s.tb_full, HALF)):
                    pe.wait_ge(c.sem, c.next())
                    for h in range(DH):
                        t = pe.transpose(bank[:, h * P:(h + 1) * P], pj[:, c0 + h * P:c0 + (h + 1) * P], ident)
                    t.then_inc(full, 1)

            def turn_rest():
                pe.wait_ge(s.tb_free, tb.next())
                for c in range(2):
                    t = pe.transpose(PB[:, c * P:(c + 1) * P], pj[:, O_PU + c * P:O_PU + (c + 1) * P], ident)
                t.then_inc(s.tb_full, 1)
                pe.wait_ge(s.ta_free, ta.next())
                pe.transpose(PA[:, 0:P], pj[:, O_LAT:O_LAT + P], ident)
                pe.transpose(PA[0:QR - P, P:2 * P], pj[:, O_LAT + P:O_LAT + QR], ident)
                pe.transpose(PA[:, 2 * P:3 * P], pj[:, O_LAT + QR:O_KR], ident).then_inc(s.ta_full, 1)

            def up_q():
                evacuated(ta)
                pe.wait_ge(s.tb_free, tb.next())
                pe.matmul(PB[:, 0:MH * MQ], latT[:, 0, :], wuq[:, 0, :], start=True, stop=False)
                pe.matmul(PB[:, 0:MH * MQ], latT[0:QR - P, 1, :], wuq[0:QR - P, 1, :],
                          start=False, stop=True).then_inc(s.tb_full, 1)

            def up_kv():
                pe.wait_ge(s.tb_free, tb.next())
                pe.matmul(PB[:, :], latT[:, 2, :], wukv[:, :], start=True, stop=True).then_inc(s.tb_full, 1)

            def turn_mla():
                pe.wait_ge(s.mla_normed, mln.next())
                for c, bank, full, src in ((ta, PA, s.ta_full, qc), (tb, PB, s.tb_full, kc)):
                    pe.wait_ge(c.sem, c.next())
                    for h in range(MH):
                        t = pe.transpose(bank[0:MQ, h * P:(h + 1) * P], src[:, h, :], ident)
                    t.then_inc(full, 1)

            def phase1():
                turn_x()
                evacuated(ta)
                evacuated(tb)
                project_first()
                pe.wait_ge(s.weights_loaded, wtl.next(4))
                turn_x()
                evacuated(ta)
                evacuated(tb)

                def body(odd, last):
                    project(0, odd)
                    turn_maps()
                    project(4, odd)
                    turn_rest()
                    project(3, odd)
                    up_q()
                    project(1, odd)
                    up_kv()
                    if not last:
                        turn_x()
                    project(2, odd)
                    turn_mla()
                steady(pe)
                with n.loop(pe, "p1", 0, NT // 2 - 1):
                    body(1, False)
                    body(0, False)
                body(1, True)
                turn_maps()
                turn_rest()
                up_q()
                up_kv()
                turn_mla()
                kept.next(5)

            def free_scores(m, c0, b0):
                if m in (10, 11):
                    pe.wait_ge(s.exp_done, expd.value(c0 + m - 1))
                elif 2 <= m < 10 or m in (14, 15):
                    pe.wait_ge(s.biased, biased.value(b0 + m - 1 if m < 10 else b0 + 8 + m - 13))
                elif m in (12, 13):
                    pe.wait_ge(s.exp_done, expd.value(c0 + m - 1))

            def scores(q, u, nxt=0, only=None):
                for m in maps(u, only):
                    free_scores(m + nxt, expd.k, biased.k)
                    for half in range(2):
                        ks = slice(half * HALF, (half + 1) * HALF)
                        if u < DH:
                            r = slice(64 * (m % 2), 64 * (m % 2) + 64)
                            t = pe.matmul(S[m % 2][:, ks], q[r, u * P:(u + 1) * P], kT[r, u, ks],
                                          start=True, stop=True)
                        else:
                            t = pe.matmul(S[m % 2][:, ks], q[0:MQ, u * P:(u + 1) * P], kmT[0:MQ, u - DH, ks],
                                          start=True, stop=True)
                    t.then_inc(s.scores_ready, 1)

            def turn_probs(u):
                if u < DH:
                    pe.wait_ge(s.mixed, mixed.next())
                else:
                    pe.wait_ge(s.exp_done, expd.value(expd.k + u + 5))
                e = (2 * u) % 4 if u < DH else u - DH
                for c, bank, full, k0 in ((tb, PB, s.tb_full, 4), (ta, PA, s.ta_full, 0)):
                    pe.wait_ge(c.sem, c.next())
                    for k in range(4):
                        t = pe.transpose(bank[:, k * P:(k + 1) * P], E[:, e, (k0 + k) * P:(k0 + k + 1) * P], ident)
                    t.then_inc(full, 1)

            def values(u, first):
                if u in (0, DH) and not first:
                    pe.wait_ge(s.x_updated, xup.next())
                evacuated(ta)
                evacuated(tb)
                o, v, w = (OD[:, u, :], V, DV) if u < DH else (OM[:, u - DH, :], VM, MV)
                c0 = (u % 4) * w
                for k in range(NT):
                    t = pe.matmul(o, AT[:, k, :], v[:, k, c0:c0 + w], start=(k == 0), stop=(k == NT - 1))
                t.then_inc(s.pv_done, 1)

            def route_tile():
                pe.wait_ge(s.hf_ready, hfr.next())
                for c, bank, full, k0 in ((tb, PB, s.tb_full, 4), (ta, PA, s.ta_full, 0)):
                    pe.wait_ge(c.sem, c.next())
                    for k in range(4):
                        t = pe.transpose(bank[:, k * P:(k + 1) * P], hf[:, (k0 + k) * P:(k0 + k + 1) * P], ident)
                    t.then_inc(full, 1)
                evacuated(ta)
                pe.wait_ge(s.tb_free, tb.next())
                for k in range(KD):
                    t = pe.matmul(PB[:, 0:NLOG], hT2[:, k, :], wr[:, k, :], start=(k == 0), stop=(k == KD - 1))
                t.then_inc(s.tb_full, 1)

            def turn_diff():
                pe.wait_ge(s.od_ready, odr.next())
                pe.wait_ge(s.ta_free, ta.next())
                for h in range(DH):
                    t = pe.transpose(PA[:, h * P:(h + 1) * P], ob[:, h * P:(h + 1) * P], ident)
                t.then_inc(s.ta_full, 1)

            def mix_pool(i, first):
                if first:
                    pe.wait_ge(s.pooled, pooled.next())
                pe.wait_ge(s.ta_free, ta.next())
                for c in range(2):
                    t = pe.matmul(PA[:, c * P:(c + 1) * P], pwd[:, c, :], put[:, c, bass.ds(i * P + PAD, P)],
                                  start=True, stop=True)
                t.then_inc(s.ta_full, 1)

            def turn_mla_out():
                pe.wait_ge(s.om_ready, omr.next())
                pe.wait_ge(s.tb_free, tb.next())
                for c in range(2):
                    t = pe.transpose(PB[:, c * P:(c + 1) * P], om[:, c * P:(c + 1) * P], ident)
                t.then_inc(s.tb_full, 1)

            def project_out():
                evacuated(ta)
                evacuated(tb)
                for half in range(2):
                    for k in range(KD):
                        t = pe.matmul(OUT[half], catT[:, k, :], wo[:, k, half * HALF:(half + 1) * HALF],
                                      start=(k == 0), stop=(k == KD - 1))
                    t.then_inc(s.out_full, 1)

            def phase2():
                def body(i, odd, first, last):
                    q, q_next = qs[odd], qs[1 - odd]
                    for u in range(8):
                        turn_probs(u)
                        if u <= 5:
                            scores(q, u + 2)
                        if u >= 6 and not last:
                            if u == 6:
                                pe.wait_ge(s.q_loaded, ql.next())
                            scores(q_next, 0, 12, u - 6)
                        values(u, first)
                        if u == 2 and not first:
                            route_tile()
                        if u == 2 and first:
                            pe.wait_ge(s.wr_loaded, wrl.next())
                        if u == 6:
                            turn_diff()
                    mix_pool(i, first)
                    turn_mla_out()
                    if not last:
                        scores(q_next, 1, 12)
                    if first:
                        pe.wait_ge(s.wo_loaded, wol.next())
                    project_out()
                    biased.next(8)
                    expd.next(12)

                pe.wait_ge(s.q_loaded, ql.next())
                scores(qs[0], 0)
                scores(qs[0], 1)
                body(0, 0, True, False)
                with n.loop(pe, "p2", 0, NT // 2 - 1) as j:
                    body(j * 2 + 1, 1, False, False)
                    body(j * 2 + 2, 0, False, False)
                body(T, 1, False, True)
                route_tile()
                xup.next(2)

            def rank_tokens():
                pe.wait_ge(s.mask_ready, masks.next())
                for i in range(NT):
                    for j in range(i + 1):
                        pe.matmul(PS[:, i * NE:(i + 1) * NE], tri[:, :] if j == i else ones[:, :], mb[:, j, :],
                                  start=(j == 0), stop=(j == i))
                for j in range(NT):
                    t = pe.matmul(PS[:, NT * NE:(NT + 1) * NE], ones[:, :], mb[:, j, :],
                                  start=(j == 0), stop=(j == NT - 1))
                t.then_inc(s.rank_full, 1)

            def slot_ids(e, r):
                pe.wait_ge(s.onehot_ready, oh.next())
                for i in range(NT):
                    t = pe.matmul(IDS[r], OH[:, r, i, :], cols[:, e, i, :], start=(i == 0), stop=(i == NT - 1))
                t.then_inc(s.ids_full, 1)

            def turn_rows(r):
                pe.wait_ge(gathered[r], gth[r].next())
                for c, bank, full, k0 in ((ta, PA, s.ta_full, 0), (tb, PB, s.tb_full, 4)):
                    pe.wait_ge(c.sem, c.next())
                    for k in range(4):
                        t = pe.transpose(bank[:, k * CAP:(k + 1) * CAP],
                                         G[0:CAP, r, k0 + k:D:KD], ident[0:CAP, 0:CAP])
                    t.then_inc(full, 1)

            def up_matmuls(w, bank):
                for f in range(2):
                    for k in range(KD):
                        t = pe.matmul(bank[:, f, :], w[:, k * FF + f * P:k * FF + (f + 1) * P], gT[:, k, :],
                                      start=(k == 0), stop=(k == KD - 1))
                return t

            def down_matmuls(w):
                for half in range(2):
                    for f in range(2):
                        t = pe.matmul(DN[:, half * HALF:(half + 1) * HALF], hh[:, f, :],
                                      w[:, f * D + half * HALF:f * D + (half + 1) * HALF],
                                      start=(f == 0), stop=(f == 1))
                return t

            def phase3():
                rank_tokens()
                slot_ids(0, 0)
                slot_ids(1, 1)
                turn_rows(0)

                def body(j, last):
                    for q in range(4):
                        r = q % 2
                        where = 4 if last and q == 3 else q
                        w = slot[where]
                        evacuated(ta)
                        evacuated(tb)
                        pe.wait_ge(wload[where], wl[where].next(3))
                        up_matmuls(w[:, 0:KD * FF], GATE).then_inc(s.gate_full, 1)
                        up_matmuls(w[:, KD * FF:2 * KD * FF], UP).then_inc(s.up_full, 1)
                        slot_ids(j * 4 + (q + 2), r)
                        turn_rows(1 - r)
                        pe.wait_ge(s.h_ready, hr.next())
                        pe.wait_ge(s.ya_ready, ya.next())
                        pe.wait_ge(s.yb_ready, yb.next())
                        down_matmuls(w[:, 2 * KD * FF:]).then_inc(s.down_full, 1)
                with n.loop(pe, "p3", 0, NE // 4 - 1) as j:
                    body(j, False)
                body(NE // 4 - 1, True)
                gth[1].next()

            pe.wait_ge(s.consts_loaded, 22)
            with pe.Fori(0, DEPTH) as layer:
                n.enter_layer(layer)
                phase1()
                barrier(pe, phase)
                phase2()
                barrier(pe, phase)
                phase3()
                barrier(pe, phase)
                overflow_tensor(pe, layer, layer + 1, up_matmuls, down_matmuls)
                barrier(pe, phase)
                n.leave_layer()

        @block.scalar
        def _(act):
            n = Counts("act")
            phase = n.on(s.phase_done, "phase")
            ta, mine, tb = n.on(s.ta_full, "ta"), n.on(s.ta_free, "mine"), n.on(s.tb_full, "tb")
            xl, pf = n.on(s.x_combined, "x"), n.on(s.proj_full, "pf")
            qst = n.on(s.q_stored, "qst", 16, DONE)
            biased, maxr, xup = n.on(s.biased, "biased"), n.on(s.max_ready, "max"), n.on(s.x_updated, "xup")
            rarg, lam = n.on(s.route_arg, "rarg"), n.on(s.lam_sum, "lam")
            gf, dn = n.on(s.gate_full, "gf"), n.on(s.down_full, "dn")
            yfree = n.on(s.y_free, "yf")
            small_r = n.on(s.small_ready, "small")

            def scaled(out_, in_, scale):
                return act.activation(out_, in_, ACT.Copy, scale=scale)

            def square_x():
                act.wait_ge(s.x_combined, xl.next())
                act.activation(xn1, xt1, ACT.Square, accum_out=st[:, 0, 20:21]).then_inc(s.x_squared, 1)

            def keep_x(odd):
                act.wait_ge(s.ta_full, ta.next())
                act.copy(hT1[odd][:, 0:4, :], PA[:, :].rearrange("p (k t) -> p k t", k=4)).then_inc(s.ta_free, 1)
                mine.next()

            def keep_projected(i, chunks):
                for c in chunks:
                    act.wait_ge(s.proj_full, pf.next())
                    w = CHUNKS[c][1]
                    dst = (pj[:, 0:HALF], pj[:, HALF:2 * HALF], V[:, i, :], pj[:, O_LAT:O_LAT + 352],
                           pj[:, O_PU:PJ])[c]
                    act.copy(dst, PS[:, c * HALF:c * HALF + w]).then_inc(s.proj_kept, 1)

            def keep_queries():
                act.wait_ge(s.ta_full, ta.next())
                act.wait_ge(s.q_stored, qst.last())
                scaled(qout[:, 0:HALF], PA[:, :], der[:, NQS:NQS + 1]).then_inc(s.ta_free, 1)
                mine.next()

            def keep_latents():
                act.wait_ge(s.ta_full, ta.next())
                scaled(latT[:, 0, :], PA[:, 0:P], cur[:, C_QL:C_QL + 1])
                scaled(latT[0:QR - P, 1, :], PA[0:QR - P, P:2 * P], cur[0:QR - P, C_QL + 1:C_QL + 2])
                scaled(latT[:, 2, :], PA[:, 2 * P:3 * P], cur[:, C_KVL:C_KVL + 1]).then_inc(s.ta_free, 1)
                mine.next()

            def keep_mla(i):
                act.wait_ge(s.ta_full, ta.next())
                scaled(qout[0:MQ, HALF:2 * HALF], PA[0:MQ, :], der[0:MQ, MQS:MQS + 1]).then_inc(s.ta_free, 1)
                act.wait_ge(s.ta_free, mine.next() + 1)
                act.dma_start(q_dram[i], qout).then_inc(s.q_stored, 16)
                qst.next()

            def phase1():
                square_x()
                keep_x(0)
                act.wait_ge(s.lam_sum, lam.next())
                act.activation(der[:, X1 + 2:X1 + 4], der[:, X1:X1 + 2], ACT.Exp).then_inc(s.lam_exp, 1)
                act.wait_ge(s.small_ready, small_r.next())
                square_x()
                keep_projected(0, ORDER)
                keep_x(1)

                def body(i, odd, last):
                    keep_queries()
                    keep_projected(i, ORDER[:1])
                    if not last:
                        square_x()
                    keep_latents()
                    keep_projected(i, ORDER[1:4])
                    if not last:
                        keep_x(1 - odd)
                    keep_projected(i, ORDER[4:])
                    keep_mla(i - 1)
                with n.loop(act, "p1", 0, NT // 2 - 1) as j:
                    body(j * 2 + 1, 1, False)
                    body(j * 2 + 2, 0, False)
                body(T, 1, True)
                keep_queries()
                keep_latents()
                keep_mla(T)
                act.wait_ge(s.q_stored, qst.last())

            def exponents(u, b0, only=None):
                for m in maps(u, only):
                    if u < DH:
                        act.wait_ge(s.biased, biased.value(b0 + m + 1))
                        act.activation(E[:, m % 4, :], SC[:, m % 2, :], ACT.Exp, scale=-1.0,
                                       bias=mn[:, m:m + 1], accum_out=rs[:, m:m + 1]).then_inc(s.exp_done, 1)
                    else:
                        act.wait_ge(s.max_ready, maxr.next())
                        act.activation(E[:, m % 4, :], S[m % 2], ACT.Exp, bias=mn[:, m:m + 1],
                                       accum_out=rs[:, m:m + 1]).then_inc(s.exp_done, 1)

            def keep_left(dst):
                act.wait_ge(s.ta_full, ta.next())
                act.copy(dst[:, 0:4, :], PA[:, :].rearrange("p (k t) -> p k t", k=4)).then_inc(s.ta_free, 1)
                mine.next()

            def phase2():
                def body(first, last):
                    for u in range(8):
                        keep_left(AT)
                        if u <= 5:
                            exponents(u + 2, biased.k)
                        if u >= 6 and not last:
                            exponents(0, biased.k + 8, u - 6)
                        if u == 2 and not first:
                            keep_left(hT2)
                        if u == 6:
                            act.wait_ge(s.ta_full, ta.next())
                            scaled(catT[:, 0:4, :], PA[:, :].rearrange("p (k t) -> p k t", k=4),
                                   der[:, NSUB:NSUB + 1]).then_inc(s.ta_free, 1)
                            mine.next()
                    act.wait_ge(s.ta_full, ta.next())
                    scaled(catT[:, 6, :], PA[:, 0:P], cur[:, C_PS:C_PS + 1])
                    scaled(catT[:, 7, :], PA[:, P:2 * P], cur[:, C_PS + 1:C_PS + 2]).then_inc(s.ta_free, 1)
                    mine.next()
                    if not last:
                        exponents(1, biased.k + 8)
                    act.wait_ge(s.x_updated, xup.next(2))
                    act.activation(junk2[:, :], xt2, ACT.Square, accum_out=st[:, 0, 20:21]).then_inc(s.x_squared, 1)
                    biased.next(8)

                exponents(0, 0)
                exponents(1, 0)
                body(True, False)
                with n.loop(act, "p2", 0, NT // 2 - 1):
                    body(False, False)
                    body(False, False)
                body(False, True)
                keep_left(hT2)

            def phase3():
                act.wait_ge(s.route_arg, rarg.next())
                act.activation(ge_[:, :, :], gv_[:, :, :], ACT.Exp).then_inc(s.route_exp, 1)
                act.wait_ge(s.route_arg, rarg.next())
                act.activation(r8[:, 5, :], r8[:, 4, :], ACT.Exp).then_inc(s.route_exp, 1)

                def keep_rows():
                    act.wait_ge(s.ta_full, ta.next())
                    act.copy(gT[:, 0:4, :], PA[:, 0:4 * CAP].rearrange("p (k t) -> p k t", k=4)).then_inc(s.ta_free, 1)
                    mine.next()
                keep_rows()
                with n.loop(act, "p3", 0, NE // 4):
                    for q in range(4):
                        r = q % 2
                        act.wait_ge(s.gate_full, gf.next())
                        act.activation(sg[:, :, :], GATE, ACT.Silu).then_inc(s.silu_ready, 1)
                        keep_rows()
                        act.wait_ge(s.down_full, dn.next())
                        act.wait_ge(s.y_free, yfree.next())
                        act.copy(Y[0:CAP, r, 0:HALF], DN[:, 0:HALF]).then_inc(s.ya_ready, 1)

            def store_output():
                for i in range(NT):
                    act.wait_ge(s.cx_ready, i + 1)
                    act.dma_start(xs[tok(i), :], c_x[i]).then_inc(s.cx_stored, 16)
                act.wait_ge(s.cx_stored, NT * 16)

            act.wait_ge(s.x_loaded, 48)
            for k in range(KD):
                act.dma_start(win[:, k, :], w_in[0, k * P:(k + 1) * P, :]).then_inc(win_loaded[k], 16)
            act.sem_inc(s.ta_free, 1)
            act.sem_inc(s.ya_ready, 1)
            act.wait_ge(s.consts_loaded, 22)
            with act.Fori(0, DEPTH) as layer:
                n.enter_layer(layer)
                phase1()
                barrier(act, phase)
                phase2()
                barrier(act, phase)
                phase3()
                barrier(act, phase)
                overflow_scalar(act, layer, layer + 1)
                barrier(act, phase)
                n.leave_layer()
            store_output()

        @block.vector
        def _(dve):
            n = Counts("dve")
            phase, step = n.on(s.phase_done, "phase"), n.on(s.step_dve, "step")
            tb, mine = n.on(s.tb_full, "tb"), n.on(s.tb_free, "mine")
            xsq, rstd, kept = n.on(s.x_squared, "xsq"), n.on(s.rstd_ready, "rstd"), n.on(s.proj_kept, "kept")
            gl, bl, lamx = n.on(s.gain_loaded, "gl", 16), n.on(s.bias_loaded, "bl", 16), n.on(s.lam_exp, "lamx")
            sr, expd, pv = n.on(s.scores_ready, "sr"), n.on(s.exp_done, "exp"), n.on(s.pv_done, "pv")
            xl, xl2, hst = n.on(s.x_loaded, "x", 48), n.on(s.x2_loaded, "x2", 16), n.on(s.h_stored, "hst", 16, DONE)
            curl = n.on(s.cur_loaded, "cur", 16)
            iol, rex = n.on(s.iota_loaded, "iota", 16), n.on(s.route_exp, "rex")
            rankf, idf = n.on(s.rank_full, "rank"), n.on(s.ids_full, "ids")
            silu, upf, dn = n.on(s.silu_ready, "silu"), n.on(s.up_full, "up"), n.on(s.down_full, "dn")
            yfree = n.on(s.y_free, "yf")
            outf = n.on(s.out_full, "out")
            smr = n.on(s.small_ready, "small")

            def do(ins):
                ins.then_inc(s.step_dve, 1)
                step.next()

            def settle():
                dve.wait_ge(s.step_dve, step.last())

            def keep(dst, src, scale=None):
                dve.wait_ge(s.tb_full, tb.next())
                if scale is None:
                    t = dve.tensor_copy(dst, src)
                else:
                    t = dve.tensor_scalar(dst, src, scale, None, ALU.mult)
                t.then_inc(s.tb_free, 1)
                mine.next()

            def bc(a, w):
                return a.unsqueeze(2).broadcast_to([a.shape[0], a.shape[1], w])

            def over(a, m):
                return a.unsqueeze(1).broadcast_to([a.shape[0], m, a.shape[1]])

            def rsqrt_asked(t):
                t.then_inc(s.var_ready, 1)
                dve.wait_ge(s.rstd_ready, rstd.next())

            def set_up_layer():
                dve.wait_ge(s.cur_loaded, curl.next())
                do(dve.tensor_scalar(der[:, NQS:NQS + 1], cur[:, C_DQG:C_DQG + 1], -(DQ ** -0.5), None, ALU.mult))
                do(dve.tensor_scalar(der[:, MQS:MQS + 1], cur[:, C_MQG:C_MQG + 1], MQ ** -0.5, None, ALU.mult))
                do(dve.tensor_tensor(der[:, NSUB:NSUB + 1], cur[:, C_SUB:C_SUB + 1], cur[:, C_LI + 1:C_LI + 2], ALU.mult))
                lv = cur[:, C_LAM:C_LAM + 4 * DQ].rearrange("p (a b d) -> p a b d", a=2, b=2)
                do(dve.tensor_tensor(rt.rearrange("p h r -> p (h r)").rearrange("p (a d) -> p a d", a=2),
                                     lv[:, :, 0, :], lv[:, :, 1, :], ALU.mult))
                settle()
                dve.tensor_reduce(der[:, X1:X1 + 2], rt.rearrange("p h r -> p (h r)").rearrange("p (a d) -> p a d", a=2),
                                  AX.X, ALU.add).then_inc(s.lam_sum, 1)
                dve.wait_ge(s.lam_exp, lamx.next())
                do(dve.tensor_tensor(der[:, X1 + 4:X1 + 5], der[:, X1 + 3:X1 + 4], der[:, X1 + 2:X1 + 3], ALU.subtract))
                settle()
                do(dve.tensor_tensor(der[:, NLAM:NLAM + 1], der[:, X1 + 4:X1 + 5], cur[:, C_LI:C_LI + 1], ALU.subtract))
                for t, (k, c) in enumerate(((K_COS, C_RGQ), (K_SIN, C_RSQ), (K_COS, C_RGK), (K_SIN, C_RSK))):
                    table = dve.tensor_tensor(rope[:, t, :, :], cst[:, k:k + NT * ROPE].rearrange("p (t r) -> p t r", t=NT),
                                              over(cur[:, c:c + ROPE], NT), ALU.mult)
                    if t < 3:
                        do(table)
                        settle()
                table.then_inc(s.small_ready, 1)
                dve.wait_ge(s.small_ready, smr.next())

            def combine_x(i):
                dve.wait_ge(s.x_loaded, xl.next())
                for k in range(2):
                    t = dve.scalar_tensor_tensor(xt1, yt1[:, k, :], gates[:, k, i:i + 1] if isinstance(i, int) else gates[:, k, bass.ds(i, 1)], xt1, ALU.mult, ALU.add)
                    if k == 0:
                        do(t)
                        settle()
                t.then_inc(s.x_combined, 1)

            def norm_x(first=False):
                dve.wait_ge(s.x_squared, xsq.next())
                rsqrt_asked(dve.tensor_scalar(st[:, 1, 20:21], st[:, 0, 20:21], 1.0 / D, EPS, ALU.mult, ALU.add))
                if first:
                    dve.wait_ge(s.gain_loaded, gl.next())
                dve.scalar_tensor_tensor(xn1, xt1, st[:, 2, 20:21], grow[:, :], ALU.mult, ALU.mult).then_inc(s.xn_ready, 1)

            def keep_x(odd):
                keep(hT1[odd][:, 4:8, :], PB[:, :].rearrange("p (k t) -> p k t", k=4))

            def keep_keys(i):
                keep(kT[:, :, tok(i)], PB[:, :].rearrange("p (h t) -> p h t", h=DH), cur[:, C_DKG:C_DKG + 1])

            def keep_pool_input(i):
                keep(put[:, :, bass.ds(i * P + PAD, P)], PB[:, 0:2 * P].rearrange("p (c t) -> p c t", c=2))

            def square_projected():
                dve.wait_ge(s.proj_kept, kept.next(4))
                kept.next()
                do(dve.tensor_tensor(sq, pj[:, 0:O_PU], pj[:, 0:O_PU], ALU.mult))

            def measure_projected():
                settle()
                for c0, c1, a, g in ((0, O_LAT, 0, 16), (O_LAT, O_LAT + QR, 16, 1), (O_LAT + QR, O_KR, 17, 1),
                                     (O_KR, O_PU, 18, 1)):
                    do(dve.tensor_reduce(st[:, 0, a:a + g], sq[:, c0:c1].rearrange("p (g d) -> p g d", g=g),
                                         AX.X, ALU.add))
                settle()
                do(dve.tensor_tensor(st[:, 0, 0:NSTAT], st[:, 0, 0:NSTAT], cst[:, K_INV:K_INV + NSTAT], ALU.mult))
                settle()
                dve.tensor_scalar(st[:, 1, 0:NSTAT], st[:, 0, 0:NSTAT], EPS, None, ALU.add).then_inc(s.var_ready, 1)

            def norm_projected(i):
                dve.wait_ge(s.rstd_ready, rstd.next())
                v = pj[:, 0:O_LAT].rearrange("p (g d) -> p g d", g=16)
                do(dve.tensor_tensor(v, v, bc(st[:, 2, 0:16], DQ), ALU.mult))
                for c0, c1, a in ((O_LAT, O_LAT + QR, 16), (O_LAT + QR, O_KR, 17), (O_KR, O_PU, 18)):
                    do(dve.tensor_scalar(pj[:, c0:c1], pj[:, c0:c1], st[:, 2, a:a + 1], None, ALU.mult))
                settle()
                kr = pj[:, O_KR:O_PU]
                do(dve.tensor_tensor(rt[:, 0, :], kr, rope[:, 2, i, :], ALU.mult))
                do(dve.tensor_tensor(rt2[:, 0, 0:16], kr[:, 16:32], rope[:, 3, i, 0:16], ALU.mult))
                do(dve.tensor_tensor(rt2[:, 0, 16:32], kr[:, 0:16], rope[:, 3, i, 16:32], ALU.mult))
                settle()
                dve.tensor_tensor(kc[:, :, NOPE:MQ], over(rt[:, 0, :], MH), over(rt2[:, 0, :], MH),
                                  ALU.add).then_inc(s.pj_normed, 1)

            def norm_mla(i, final=False):
                dve.wait_ge(s.tb_free, mine.last() + 1)
                nq = MH * MQ
                do(dve.tensor_tensor(sq[:, 0:nq + HALF], mj, mj, ALU.mult))
                q, k = mj[:, 0:nq].rearrange("p (h d) -> p h d", h=MH), mj[:, nq:].rearrange("p (h d) -> p h d", h=MH)
                q2, k2 = (sq[:, 0:nq].rearrange("p (h d) -> p h d", h=MH),
                          sq[:, nq:nq + HALF].rearrange("p (h d) -> p h d", h=MH))
                do(dve.tensor_copy(VM[:, i, :].rearrange("p (h d) -> p h d", h=MH), k[:, :, NOPE:NOPE + MV]))
                settle()
                do(dve.tensor_reduce(st[:, 0, 0:4], q2[:, :, 0:NOPE], AX.X, ALU.add))
                do(dve.tensor_reduce(st[:, 0, 4:8], q2[:, :, NOPE:MQ], AX.X, ALU.add))
                do(dve.tensor_reduce(st[:, 0, 8:12], k2[:, :, 0:NOPE], AX.X, ALU.add))
                settle()
                do(dve.tensor_tensor(st[:, 0, 0:12], st[:, 0, 0:12], cst[:, K_INV2:K_INV2 + 12], ALU.mult))
                settle()
                dve.tensor_scalar(st[:, 1, 0:12], st[:, 0, 0:12], EPS, None, ALU.add).then_inc(s.var_ready, 1)
                if not final:
                    square_projected()
                dve.wait_ge(s.rstd_ready, rstd.next())
                do(dve.tensor_tensor(qc[:, :, 0:NOPE], q[:, :, 0:NOPE], bc(st[:, 2, 0:4], NOPE), ALU.mult))
                do(dve.tensor_tensor(kc[:, :, 0:NOPE], k[:, :, 0:NOPE], bc(st[:, 2, 8:12], NOPE), ALU.mult))
                do(dve.tensor_tensor(q[:, :, NOPE:MQ], q[:, :, NOPE:MQ], bc(st[:, 2, 4:8], ROPE), ALU.mult))
                settle()
                do(dve.tensor_tensor(rt[:, :, :], q[:, :, NOPE:MQ], over(rope[:, 0, i, :], MH), ALU.mult))
                do(dve.tensor_tensor(rt2[:, :, 0:16], q[:, :, NOPE + 16:MQ], over(rope[:, 1, i, 0:16], MH), ALU.mult))
                do(dve.tensor_tensor(rt2[:, :, 16:32], q[:, :, NOPE:NOPE + 16], over(rope[:, 1, i, 16:32], MH), ALU.mult))
                settle()
                dve.tensor_tensor(qc[:, :, NOPE:MQ], rt[:, :, :], rt2[:, :, :], ALU.add).then_inc(s.mla_normed, 1)

            def keep_mla_in():
                keep(mj[:, 0:MH * MQ], PB[:, 0:MH * MQ])
                keep(mj[:, MH * MQ:], PB[:, :])

            def keep_mla(i):
                keep(kmT[0:MQ, :, tok(i)], PB[0:MQ, :].rearrange("p (h t) -> p h t", h=MH), cur[0:MQ, C_MKG:C_MKG + 1])

            def phase1():
                combine_x(0)
                norm_x(True)
                keep_x(0)
                set_up_layer()
                combine_x(1)
                norm_x()
                keep_x(1)
                square_projected()
                measure_projected()
                norm_projected(0)

                def body(i, odd, last):
                    keep_keys(i - 1)
                    if not last:
                        combine_x(i + 1)
                    keep_pool_input(i - 1)
                    if not last:
                        norm_x()
                    keep_mla_in()
                    if not last:
                        keep_x(1 - odd)
                    norm_mla(i - 1)
                    measure_projected()
                    keep_mla(i - 1)
                    norm_projected(i)
                with n.loop(dve, "p1", 0, NT // 2 - 1) as j:
                    body(j * 2 + 1, 1, False)
                    body(j * 2 + 2, 0, False)
                body(T, 1, True)
                keep_keys(T)
                keep_pool_input(T)
                keep_mla_in()
                norm_mla(T, True)
                keep_mla(T)

            def bias_scores(u, c0, nxt=0, only=None):
                if u == 0 and not only:
                    dve.wait_ge(s.bias_loaded, bl.next())
                for m in maps(u, only):
                    dve.wait_ge(s.scores_ready, sr.next())
                    if u < DH:
                        if m >= 2:
                            dve.wait_ge(s.exp_done, expd.value(c0 + nxt + m - 1))
                        steady(dve)
                        dve.tensor_tensor_reduce(SC[:, m % 2, :], S[m % 2], bias[:, u, :],
                                                 1.0, 3.0e38, ALU.add, ALU.min, mn[:, m:m + 1]).then_inc(s.biased, 1)
                    else:
                        dve.tensor_reduce(mn[:, m:m + 1], S[m % 2], AX.X, ALU.max, negate=True).then_inc(s.max_ready, 1)

            def mix(u, c0, nxt=0):
                if u < DH:
                    dve.wait_ge(s.exp_done, expd.value(c0 + nxt + 2 * u + 2))
                    do(dve.reciprocal(rc[:, 2 * u:2 * u + 2], rs[:, 2 * u:2 * u + 2]))
                    settle()
                    do(dve.tensor_scalar(cf[:, u:u + 1], rs[:, 2 * u:2 * u + 1], rc[:, 2 * u + 1:2 * u + 2],
                                         der[:, NLAM:NLAM + 1], ALU.mult, ALU.mult))
                    settle()
                    e = (2 * u) % 4
                    dve.scalar_tensor_tensor(E[:, e, :], E[:, e + 1, :], cf[:, u:u + 1], E[:, e, :],
                                             ALU.mult, ALU.add).then_inc(s.mixed, 1)
                else:
                    dve.wait_ge(s.exp_done, expd.value(c0 + nxt + u + 5))
                    do(dve.reciprocal(rc[:, u + 4:u + 5], rs[:, u + 4:u + 5]))

            def keep_right(dst):
                keep(dst[:, 4:8, :], PB[:, :].rearrange("p (k t) -> p k t", k=4))

            def variance_x():
                dve.wait_ge(s.x_squared, xsq.next())
                dve.tensor_scalar(st[:, 1, 20:21], st[:, 0, 20:21], 1.0 / D, EPS, ALU.mult, ALU.add).then_inc(s.var_ready, 1)

            def norm_x2():
                dve.wait_ge(s.rstd_ready, rstd.next())
                dve.wait_ge(s.h_stored, hst.last())
                hst.next()
                dve.scalar_tensor_tensor(hf, xt2, st[:, 2, 20:21], grow[:, :], ALU.mult, ALU.mult).then_inc(s.hf_ready, 1)

            def keep_routed(i):
                keep_right(hT2)
                dve.wait_ge(s.tb_full, tb.next())
                dve.tensor_tensor(logits[:, i, :], PB[:, 0:NLOG], cur[:, C_RB:C_RB + NLOG], ALU.add).then_inc(s.tb_free, 1)
                mine.next()

            def norm_diff_start():
                dve.wait_ge(s.pv_done, pv.value(pv.k + 4))
                o3, q3 = ob.rearrange("p (h d) -> p h d", h=DH), osq.rearrange("p (h d) -> p h d", h=DH)
                do(dve.tensor_tensor(o3, OD, bc(rc[:, 0:8:2], DV), ALU.mult))
                settle()
                do(dve.tensor_tensor(q3, o3, o3, ALU.mult))
                settle()
                do(dve.tensor_reduce(st[:, 0, 12:16], q3, AX.X, ALU.add))
                settle()
                dve.tensor_scalar(st[:, 1, 12:16], st[:, 0, 12:16], 1.0 / DV, EPS, ALU.mult, ALU.add).then_inc(s.var_ready, 1)

            def norm_diff_end():
                dve.wait_ge(s.rstd_ready, rstd.next())
                o3 = ob.rearrange("p (h d) -> p h d", h=DH)
                dve.tensor_tensor(o3, o3, bc(st[:, 2, 12:16], DV), ALU.mult).then_inc(s.od_ready, 1)

            def phase2():
                def body(i, first, last):
                    c0 = expd.k
                    for u in range(8):
                        keep_right(AT)
                        if u <= 6:
                            mix(u + 1, c0)
                        if u <= 5:
                            bias_scores(u + 2, c0)
                        if u >= 6 and not last:
                            bias_scores(0, c0, 12, u - 6)
                        if not first:
                            if u == 0:
                                variance_x()
                            if u == 1:
                                norm_x2()
                            if u == 2:
                                keep_routed(i - 1)
                        if u == 4:
                            norm_diff_start()
                        if u == 5:
                            norm_diff_end()
                    dve.wait_ge(s.pv_done, pv.next(8))
                    settle()
                    dve.tensor_tensor(om.rearrange("p (h d) -> p h d", h=MH), OM, bc(rc[:, 8:12], MV),
                                      ALU.mult).then_inc(s.om_ready, 1)
                    keep(catT[:, 4:6, :], PB[:, 0:2 * P].rearrange("p (c t) -> p c t", c=2))
                    if not last:
                        bias_scores(1, c0, 12)
                        mix(0, c0, 12)
                    dve.wait_ge(s.x2_loaded, xl2.next())
                    for half in range(2):
                        ks = slice(half * HALF, (half + 1) * HALF)
                        dve.wait_ge(s.out_full, outf.next())
                        dve.tensor_tensor(xt2[:, ks], OUT[half], xt2[:, ks], ALU.add).then_inc(s.x_updated, 1)
                    expd.next(12)

                bias_scores(0, 0)
                bias_scores(1, 0)
                mix(0, 0)
                body(0, True, False)
                dve.wait_ge(s.gain_loaded, gl.next())
                steady(dve)
                with n.loop(dve, "p2", 0, NT // 2 - 1) as j:
                    body(j * 2 + 1, False, False)
                    body(j * 2 + 2, False, False)
                body(T, False, True)
                variance_x()
                norm_x2()
                keep_routed(T)

            def least_index(mask, val, values, best, w):
                do(dve.tensor_tensor(mask, values, bc(best, w), ALU.is_equal))
                settle()
                i8 = cst[:, K_I8:K_I8 + w].unsqueeze(1).broadcast_to([P, NT, w])
                do(dve.scalar_tensor_tensor(val, mask, -16.0, i8, ALU.mult, ALU.add))
                settle()
                do(dve.tensor_reduce(r8[:, 15, :], val, AX.X, ALU.min))
                settle()
                do(dve.tensor_tensor(mask, val, bc(r8[:, 15, :], w), ALU.is_equal))
                settle()

            def route():
                settle()
                dve.wait_ge(s.tb_free, mine.last() + 1)
                GL, EL = logits[:, :, 0:NG], logits[:, :, NG:NLOG]
                do(dve.tensor_reduce(r8[:, 0, :], GL, AX.X, ALU.max))
                settle()
                dve.tensor_tensor(gv_, GL, bc(r8[:, 0, :], NG), ALU.subtract).then_inc(s.route_arg, 1)
                least_index(gm_, gk_, GL, r8[:, 0, :], NG)
                dve.wait_ge(s.route_exp, rex.next())
                do(dve.tensor_reduce(r8[:, 1, :], ge_, AX.X, ALU.add))
                m4 = mb1.rearrange("p t (g e) -> p t g e", g=NG)
                do(dve.tensor_tensor(m4, EL.rearrange("p t (g e) -> p t g e", g=NG),
                                     gm_.unsqueeze(3).broadcast_to([P, NT, NG, EPG]), ALU.mult))
                settle()
                do(dve.tensor_reduce(es, mb1.rearrange("p t (g e) -> p t e g", g=NG), AX.X, ALU.add))
                settle()
                do(dve.tensor_reduce(r8[:, 2, :], es, AX.X, ALU.max))
                settle()
                least_index(ek1, ev, es, r8[:, 2, :], EPG)
                do(dve.scalar_tensor_tensor(es, ek1, -1.0e30, es, ALU.mult, ALU.add))
                settle()
                do(dve.tensor_reduce(r8[:, 3, :], es, AX.X, ALU.max))
                settle()
                dve.tensor_tensor(r8[:, 4, :], r8[:, 3, :], r8[:, 2, :], ALU.subtract).then_inc(s.route_arg, 1)
                least_index(ek2, ev, es, r8[:, 3, :], EPG)
                g4 = gm_.unsqueeze(3).broadcast_to([P, NT, NG, EPG])
                for m, ek in ((mb1, ek1), (mb2, ek2)):
                    do(dve.tensor_tensor(m.rearrange("p t (g e) -> p t g e", g=NG), g4,
                                         ek.unsqueeze(2).broadcast_to([P, NT, NG, EPG]), ALU.mult))
                settle()
                do(dve.tensor_tensor(mb1, mb1, mb2, ALU.add))
                settle()
                dve.tensor_copy(mb, mb1).then_inc(s.mask_ready, 1)
                dve.wait_ge(s.route_exp, rex.next())
                do(dve.reciprocal(r8[:, 6, :], r8[:, 1, :]))
                do(dve.tensor_scalar(r8[:, 7, :], r8[:, 5, :], 1.0, None, ALU.add))
                settle()
                do(dve.reciprocal(r8[:, 8, :], r8[:, 7, :]))
                settle()
                do(dve.tensor_tensor(gates[:, 0, :], r8[:, 6, :], r8[:, 8, :], ALU.mult))
                settle()
                do(dve.tensor_tensor(gates[:, 1, :], gates[:, 0, :], r8[:, 5, :], ALU.mult))
                do(dve.tensor_scalar(cols[:, 0:NE, :, 2], mb2.rearrange("p t e -> p e t"), float(SEQ), -float(OOB),
                                     ALU.mult, ALU.add))
                do(dve.memset(cols[:, NE:NE + 2, :, 2], 0.0))
                do(dve.tensor_copy(cols[:, :, :, 0], cst[:, K_TILE:K_TILE + NT].unsqueeze(1).broadcast_to([P, NE + 2, NT])))
                do(dve.tensor_copy(cols[:, :, :, 1], cst[:, K_P:K_P + 1].unsqueeze(2).broadcast_to([P, NE + 2, NT])))
                do(dve.memset(rank[:, NE:NE + 2, :], -1.0))
                dve.wait_ge(s.rank_full, rankf.next())
                do(dve.scalar_tensor_tensor(big, PS[:, 0:NT * NE].rearrange("p (t e) -> p t e", t=NT), 1.0, mb1,
                                            ALU.add, ALU.mult))
                settle()
                do(dve.tensor_scalar(rank[:, 0:NE, :].rearrange("p e t -> p t e"), big, -1.0, None, ALU.add))
                dve.tensor_reduce(nmax[:, :], PS[:, NT * NE:(NT + 1) * NE], AX.X, ALU.max).then_inc(s.nmax_ready, 1)
                settle()

            def onehot(e, r):
                dve.tensor_tensor(OH[:, r, :, :], iota[:, 0:CAP].unsqueeze(1).broadcast_to([P, NT, CAP]),
                                  bc(rank[:, e, :], CAP), ALU.is_equal).then_inc(s.onehot_ready, 1)

            def slot_ids(q, r):
                dve.wait_ge(s.ids_full, idf.next())
                do(dve.tensor_reduce(eids[0:CAP, q, 0:1], IDS[r][:, 0:2], AX.X, ALU.add))
                settle()
                dve.scalar_tensor_tensor(eids[0:CAP, q, 1:2], IDS[r][:, 2:3], float(OOB), eids[0:CAP, q, 0:1],
                                         ALU.add, ALU.add).then_inc(s.ids_ready, 1)

            def keep_rows():
                keep(gT[:, 4:8, :], PB[:, 0:4 * CAP].rearrange("p (k t) -> p k t", k=4))

            def phase3():
                route()
                dve.wait_ge(s.iota_loaded, iol.next())
                onehot(0, 0)
                onehot(1, 1)
                slot_ids(0, 0)
                slot_ids(1, 1)
                keep_rows()
                with n.loop(dve, "p3", 0, NE // 4) as j:
                    for q in range(4):
                        r = q % 2
                        onehot(j * 4 + (q + 2), r)
                        dve.wait_ge(s.silu_ready, silu.next())
                        dve.wait_ge(s.up_full, upf.next())
                        dve.tensor_tensor(hh[:, :, :], sg[:, :, :], UP, ALU.mult).then_inc(s.h_ready, 1)
                        dve.wait_ge(s.y_free, yfree.next())
                        slot_ids((q + 2) % 4, r)
                        keep_rows()
                        dve.wait_ge(s.down_full, dn.next())
                        dve.tensor_copy(Y[0:CAP, r, HALF:D], DN[:, HALF:D]).then_inc(s.yb_ready, 1)

            def combine_output():
                dve.wait_ge(s.held_loaded, NT * 16)
                for i in range(NT):
                    r = i % RING
                    dve.wait_ge(cy_loaded[r], (i // RING + 1) * 32)
                    for k, done in enumerate((s.cx_half, s.cx_ready)):
                        dve.scalar_tensor_tensor(c_x[i], c_y[:, 2 * r + k, :], gates[:, k, i:i + 1], c_x[i],
                                                 ALU.mult, ALU.add).then_inc(done, 1)
                        if k == 0:
                            dve.wait_ge(s.cx_half, i + 1)

            dve.sem_inc(s.tb_free, 1)
            dve.sem_inc(s.yb_ready, 1)
            dve.memset(yt1[:, :, :], 0.0).then_inc(s.consts_loaded, 1)
            dve.memset(gates[:, :, :], 0.0).then_inc(s.consts_loaded, 1)
            dve.memset(qout[MQ:P, HALF:2 * HALF], 0.0).then_inc(s.consts_loaded, 1)
            dve.wait_ge(s.consts_loaded, 20)
            dve.tensor_copy(tri[:, :], cst[:, K_TRI:K_TRI + P]).then_inc(s.consts_loaded, 1)
            dve.memset(ones[:, :], 1.0).then_inc(s.consts_loaded, 1)
            dve.wait_ge(s.consts_loaded, 22)
            with dve.Fori(0, DEPTH) as layer:
                n.enter_layer(layer)
                phase1()
                barrier(dve, phase)
                phase2()
                barrier(dve, phase)
                phase3()
                barrier(dve, phase)
                overflow_vector(dve, layer, layer + 1)
                barrier(dve, phase)
                n.leave_layer()
            combine_output()

        @block.gpsimd
        def _(pool):
            n = Counts("pool")
            phase, step = n.on(s.phase_done, "phase"), n.on(s.step_pool, "step")
            var = n.on(s.var_ready, "var")
            inv, idr = n.on(s.inv_loaded, "inv", 16), n.on(s.ids_ready, "ids")
            ya, yb = n.on(s.ya_ready, "ya"), n.on(s.yb_ready, "yb")
            sct = [n.on(scattered[r], f"s{r}", 16) for r in range(2)]

            gth = [n.on(gathered[r], f"g{r}", 16) for r in range(2)]

            def rsqrt(c0, w):
                pool.wait_ge(s.var_ready, var.next())
                pool.tensor_tensor(st[:, 2, c0:c0 + w], st[:, 1, c0:c0 + w], cst[:, K_NH:K_NH + w],
                                   ALU.pow).then_inc(s.rstd_ready, 1)

            def do(ins):
                ins.then_inc(s.step_pool, 1)
                pool.wait_ge(s.step_pool, step.next())
                steady(pool)

            def pool_windows():
                lo, hi = slice(0, 64), slice(64, P)
                add = lambda o, a, b: do(pool.tensor_tensor(o, a, b, ALU.add))
                N = PAD + SEQ + PAD
                add(pool_a[:, :, 1:N], put[:, :, 0:N - 1], put[:, :, 1:N])
                add(pool_b[hi, 0, 2:N - 1], pool_a[hi, 0, 1:N - 2], pool_a[hi, 0, 3:N])
                add(pool_b[:, 1, 2:N - 1], pool_a[:, 1, 1:N - 2], pool_a[:, 1, 3:N])
                add(pool_a[:, 1, 4:N - 3], pool_b[:, 1, 2:N - 5], pool_b[:, 1, 6:N - 1])
                add(pool_b[hi, 1, 8:N - 7], pool_a[hi, 1, 4:N - 11], pool_a[hi, 1, 12:N - 3])
                pool.wait_ge(s.inv_loaded, inv.next(4))
                for c in range(2):
                    for part, buf in ((lo, pool_a), (hi, pool_b)):
                        w, u = buf[part, c, PAD:PAD + SEQ], put[part, c, PAD:PAD + SEQ]
                        do(pool.tensor_tensor(w, w, invc[part, c, :], ALU.mult))
                        do(pool.tensor_tensor(u, w, u, ALU.subtract))
                pool.sem_inc(s.pooled, 1)

            def phase1():
                rsqrt(20, 1)
                rsqrt(20, 1)
                rsqrt(0, NSTAT)

                def body(last):
                    if not last:
                        rsqrt(20, 1)
                    rsqrt(0, 12)
                    rsqrt(0, NSTAT)
                with n.loop(pool, "p1", 0, NT // 2 - 1):
                    body(False)
                    body(False)
                body(True)
                rsqrt(0, 12)

            def phase2():
                def body(first, last):
                    if first:
                        pool_windows()
                    else:
                        rsqrt(20, 1)
                    rsqrt(12, 4)
                body(True, False)
                with n.loop(pool, "p2", 1, T):
                    body(False, False)
                body(False, True)
                rsqrt(20, 1)

            def phase3():
                def gather(q, r):
                    pool.wait_ge(s.ids_ready, idr.next())
                    gather_rows(pool, q, r).then_inc(gathered[r], 16)
                    gth[r].next()
                gather(0, 0)
                gather(1, 1)

                def body(first):
                    for q in range(4):
                        r = q % 2
                        gather((q + 2) % 4, r)
                        pool.wait_ge(s.ya_ready, ya.next() + 1)
                        pool.wait_ge(s.yb_ready, yb.next() + 1)
                        scatter_rows(pool, q, r).then_inc(scattered[r], 16)
                        sct[r].next()
                        if not (first and q == 0):
                            pool.wait_ge(scattered[1 - r], sct[1 - r].last())
                            pool.sem_inc(s.y_free, 1)
                body(True)
                with n.loop(pool, "p3", 1, NE // 4):
                    body(False)
                pool.wait_ge(scattered[1], sct[1].last())
                pool.sem_inc(s.y_free, 1)
                for r in range(2):
                    pool.wait_ge(gathered[r], gth[r].last())

            pool.memset(put[:, :, :], 0.0).then_inc(s.consts_loaded, 1)
            pool.wait_ge(s.consts_loaded, 22)
            with pool.Fori(0, DEPTH) as layer:
                n.enter_layer(layer)
                phase1()
                barrier(pool, phase)
                phase2()
                barrier(pool, phase)
                phase3()
                barrier(pool, phase)
                overflow_gpsimd(pool, layer, layer + 1)
                barrier(pool, phase)
                n.leave_layer()

        @block.sync
        def _(sp):
            n = Counts("sp")
            phase = n.on(s.phase_done, "phase")
            xn, sr, bsd = n.on(s.xn_ready, "xn"), n.on(s.scores_ready, "sr"), n.on(s.biased, "biased")
            xup, hfr = n.on(s.x_updated, "xup"), n.on(s.hf_ready, "hf")
            xst, hst = n.on(s.x_stored, "xst", 16, DONE), n.on(s.h_stored, "hst", 16, DONE)
            pooled, dn = n.on(s.pooled, "pooled"), n.on(s.down_full, "dn")
            xc, pvd = n.on(s.x_combined, "xc"), n.on(s.pv_done, "pv")
            gth = n.on(gathered[1], "g1", 16)
            qst, keptc = n.on(s.q_stored, "qst", 16, DONE), n.on(s.proj_kept, "kept")

            def load_bias(i):
                sp.dma_start(bias, alibi[:, :, bass.ds((NT - 1 - i) * P, SEQ)]).then_inc(s.bias_loaded, 16)

            def load_x(layer, i):
                with sp.If(layer > 0):
                    sp.dma_start(xt1, xs[tok(i), :]).then_inc(s.x_loaded, 16)
                    for k in range(2):
                        sp.dma_start(yt1[:, k, :], y_dram[bass.ds(k * SEQ + i * P, P), :]).then_inc(s.x_loaded, 16)
                with sp.Else():
                    sp.dma_start(xt1, x[0, tok(i), :]).then_inc(s.x_loaded, 16)
                    sp.sem_inc(s.x_loaded, 32)

            def store_x(i):
                sp.wait_ge(s.x_combined, xc.next())
                steady(sp)
                sp.dma_start(xs[tok(i), :], xt1).then_inc(s.x_stored, 16)
                xst.next()

            def phase1(layer):
                load_x(layer, 0)
                sp.dma_start(grow[:, :], gain_rows[layer, 0]).then_inc(s.gain_loaded, 16)
                sp.dma_start(wuq[:, 0, :], w_uq[layer, 0:P, :]).then_inc(s.weights_loaded, 16)
                sp.dma_start(wuq[0:QR - P, 1, :], w_uq[layer, P:QR, :]).then_inc(s.weights_loaded, 16)
                sp.dma_start(wukv[:, :], w_ukv[layer]).then_inc(s.weights_loaded, 16)
                sp.dma_start(pwd[:, :, :], pool_w[layer]).then_inc(s.weights_loaded, 16)
                sp.dma_start(wr[:, :, :], w_router[layer]).then_inc(s.wr_loaded, 16)
                with n.loop(sp, "p1", 1, NT) as i:
                    store_x(i - 1)
                    sp.wait_ge(s.xn_ready, xn.next())
                    steady(sp)
                    sp.wait_ge(s.x_stored, xst.last())
                    steady(sp)
                    load_x(layer, i)
                store_x(T)
                sp.wait_ge(s.xn_ready, xn.next())
                steady(sp)
                sp.wait_ge(s.x_stored, xst.last())
                steady(sp)
                sp.wait_ge(s.q_stored, qst.last() + DONE)
                steady(sp)
                qst.next(NT)
                sp.dma_start(qs[0], q_dram[0]).then_inc(s.q_loaded, 16)
                sp.wait_ge(s.proj_kept, keptc.next(5 * NT))
                steady(sp)
                load_bias(0)
                for c in range(2):
                    for h, part in enumerate((slice(0, 64), slice(64, P))):
                        sp.dma_start(invc[part, c, :], inv_count[2 * c + h]).then_inc(s.inv_loaded, 16)
                sp.dma_start(wo, w_out[layer].rearrange("(k p) n -> p k n", p=P)).then_inc(s.wo_loaded, 16)

            def phase2(layer):
                sp.dma_start(xt2, xs[0:P, :]).then_inc(s.x2_loaded, 16)
                sp.dma_start(grow[:, :], gain_rows[layer, 1]).then_inc(s.gain_loaded, 16)

                def finish_h(i):
                    sp.wait_ge(s.hf_ready, hfr.next())
                    steady(sp)
                    sp.dma_start(h_dram[tok(i), :], hf).then_inc(s.h_stored, 16)
                    hst.next()

                def finish_x(i):
                    sp.wait_ge(s.x_updated, xup.next(2))
                    steady(sp)
                    sp.dma_start(xs[tok(i), :], xt2).then_inc(s.x_stored, 16)
                    xst.next()

                def body(i, odd, first, last):
                    if not last:
                        sp.wait_ge(s.scores_ready, sr.last() + 1)
                        steady(sp)
                        sp.dma_start(qs[1 - odd], q_dram[i + 1]).then_inc(s.q_loaded, 16)
                    if not first:
                        finish_h(i - 1)
                        sp.wait_ge(s.x_stored, xst.last())
                        steady(sp)
                        sp.dma_start(xt2, xs[tok(i), :]).then_inc(s.x2_loaded, 16)
                    if not last:
                        sp.wait_ge(s.biased, bsd.next(8))
                        steady(sp)
                        load_bias(i + 1)
                    else:
                        bsd.next(8)
                    sp.wait_ge(s.scores_ready, sr.next(12))
                    steady(sp)
                    if last:
                        sp.wait_ge(s.pv_done, pvd.last() + DH)
                        steady(sp)
                        for q in (2, 3):
                            load_expert(sp, layer, q, q, wload[q])
                    pvd.next(8)
                    finish_x(i)
                body(0, 0, True, False)
                sp.wait_ge(s.pooled, pooled.next())
                steady(sp)
                load_expert(sp, layer, 0, 0, wload[0])
                with n.loop(sp, "p2", 0, NT // 2 - 1) as j:
                    body(j * 2 + 1, 1, False, False)
                    body(j * 2 + 2, 0, False, False)
                body(T, 1, False, True)
                finish_h(T)
                sp.wait_ge(s.x_stored, xst.last())
                steady(sp)
                sp.wait_ge(s.h_stored, hst.last())
                steady(sp)

            def load_next(layer, before):
                sp.dma_start(cur[:, :], small[layer]).then_inc(s.cur_loaded, 16)
                for ks, used in (((0, 1), before[0]), ((2, 3, 4), before[1]), ((5, 6, 7), before[3])):
                    sp.wait_ge(s.down_full, used)
                    steady(sp)
                    for k in ks:
                        sp.dma_start(win[:, k, :], w_in[layer, k * P:(k + 1) * P, :]).then_inc(win_loaded[k], 16)

            def phase3(layer):
                sp.dma_start(iota, slots_iota).then_inc(s.iota_loaded, 16)
                load_expert(sp, layer, 1, 1, wload[1])
                sp.wait_ge(gathered[1], gth.next())
                steady(sp)
                gth.next(NE // 2)
                load_expert(sp, layer, NE - 1, 4, wload[4])

                def body(j, last):
                    for q in range(3 if last else 4):
                        sp.wait_ge(s.down_full, dn.next())
                        steady(sp)
                        load_expert(sp, layer, j * 4 + q, q, wload[q])
                with n.loop(sp, "p3", 1, NE // 4 - 1) as j:
                    body(j, False)
                body(NE // 4 - 1, True)
                dn.next()
                before = dn.next(), dn.next(), dn.next(), dn.next()
                for nxt in range(1, DEPTH):
                    with sp.If(layer == nxt - 1):
                        load_next(nxt, before)
                with sp.If(layer > DEPTH - 2):
                    for tiles, used in ((range(SLOT // D), before[0]), (range(SLOT // D, NT), before[1])):
                        sp.wait_ge(s.down_full, used)
                        steady(sp)
                        for i in tiles:
                            sp.dma_start(c_x[i], xs[tok(i), :]).then_inc(s.held_loaded, 16)

            def load_outputs():
                for i in range(NT):
                    r = i % RING
                    if i >= RING:
                        sp.wait_ge(s.cx_ready, i - RING + 1)
                    for k in range(2):
                        sp.dma_start(c_y[:, 2 * r + k, :], y_dram[k * SEQ + i * P:k * SEQ + (i + 1) * P, :]).then_inc(cy_loaded[r], 16)

            for ring in (s.x_stored, s.h_stored, s.q_stored):
                sp.sem_inc(ring, DONE)
            sp.sem_inc(s.y_free, 2)
            sp.sem_inc(s.o_free, 1)
            sp.dma_start(cst[:, :], consts).then_inc(s.consts_loaded, 16)
            sp.dma_start(cur[:, :], small[0]).then_inc(s.cur_loaded, 16)
            with sp.Fori(0, DEPTH) as layer:
                n.enter_layer(layer)
                phase1(layer)
                barrier(sp, phase)
                phase2(layer)
                barrier(sp, phase)
                phase3(layer)
                barrier(sp, phase)
                overflow_sync(sp, layer, layer + 1)
                barrier(sp, phase)
                n.leave_layer()
            load_outputs()


def kernel(x, norm1_g, w_in, diff_q_norm_g, diff_k_norm_g, diff_lambda, diff_sub_norm_g,
           mla_q_lat_norm_g, mla_kv_lat_norm_g, mla_w_uq, mla_w_ukv,
           mla_q_nope_norm_g, mla_q_rope_norm_g, mla_k_nope_norm_g, mla_k_rope_norm_g,
           pool_w, pool_scale, w_out, norm2_g,
           router_group_w, router_group_b, router_expert_w, router_expert_b,
           expert_w_gate, expert_w_up, expert_w_down):
    import numpy as np
    import concourse.bacc as bacc
    from concourse.bass_utils import run_bass_kernel_spmd

    f = np.float32
    L_ = DEPTH
    small = np.zeros((P, L_, N_SM), f)
    rows = lambda a: np.broadcast_to(np.asarray(a)[None], (P,) + np.asarray(a).shape)
    for h in range(2):
        small[h * 64:h * 64 + 64, :, C_DQG] = np.asarray(diff_q_norm_g).T
        small[h * 64:h * 64 + 64, :, C_DKG] = np.asarray(diff_k_norm_g).T
    small[:, :, C_SUB] = np.asarray(diff_sub_norm_g).T
    small[:, :, C_QL] = np.asarray(mla_q_lat_norm_g)[:, 0:P].T
    small[0:QR - P, :, C_QL + 1] = np.asarray(mla_q_lat_norm_g)[:, P:QR].T
    small[:, :, C_KVL] = np.asarray(mla_kv_lat_norm_g).T
    small[0:NOPE, :, C_MQG] = np.asarray(mla_q_nope_norm_g).T
    small[NOPE:MQ, :, C_MQG] = 1.0
    small[0:NOPE, :, C_MKG] = np.asarray(mla_k_nope_norm_g).T
    small[NOPE:MQ, :, C_MKG] = 1.0
    for c in range(2):
        small[:, :, C_PS + c] = np.asarray(pool_scale)[:, c * P:(c + 1) * P].T
    for c, g in ((C_RGQ, mla_q_rope_norm_g), (C_RGK, mla_k_rope_norm_g)):
        g = np.asarray(g)
        small[:, :, c:c + ROPE] = rows(g)
        small[:, :, c + ROPE:c + ROPE + 16] = rows(g[:, 16:32])
        small[:, :, c + ROPE + 16:c + 2 * ROPE] = rows(g[:, 0:16])
    small[:, :, C_RB:C_RB + NG] = rows(router_group_b)
    small[:, :, C_RB + NG:C_RB + NLOG] = rows(router_expert_b)
    small[:, :, C_LAM:C_LAM + 4 * DQ] = rows(np.asarray(diff_lambda).reshape(L_, 4 * DQ))
    for layer in range(L_):
        lam_init = 0.8 - 0.6 * math.exp(-0.3 * layer)
        small[:, layer, C_LI] = lam_init
        small[:, layer, C_LI + 1] = 1.0 - lam_init
    gain_rows = np.ascontiguousarray(np.broadcast_to(
        np.stack([np.asarray(norm1_g), np.asarray(norm2_g)], axis=1)[:, :, None, :], (L_, 2, P, D)))
    pw = np.zeros((L_, P, 2, P), f)
    for g in range(4):
        h = 64 * (g % 2)
        pw[:, h:h + 64, g // 2, h:h + 64] = np.asarray(pool_w)[:, g]
    wr = np.ascontiguousarray(np.concatenate([np.asarray(router_group_w), np.asarray(router_expert_w)], axis=2)
                              .reshape(L_, KD, P, NLOG).transpose(0, 2, 1, 3))
    cst = np.zeros((P, N_K), f)
    cst[:, K_ID:K_ID + P] = np.eye(P)
    inv = (1.0 / (10000.0 ** (np.arange(0, ROPE, 2, dtype=f) / ROPE))).astype(f)
    ang = (np.arange(SEQ, dtype=f)[:, None] * inv[None, :]).astype(f)
    for k, a in ((K_COS, (np.cos(ang), np.cos(ang))), (K_SIN, (-np.sin(ang), np.sin(ang)))):
        t = np.concatenate(a, axis=1).astype(f).reshape(NT, P, ROPE).transpose(1, 0, 2)
        cst[:, k:k + NT * ROPE] = t.reshape(P, NT * ROPE)
    cst[:, K_INV:K_INV + NSTAT] = [1 / DQ] * 16 + [1 / QR, 1 / KVR, 1 / ROPE]
    cst[:, K_INV2:K_INV2 + 12] = [1 / NOPE] * 4 + [1 / ROPE] * 4 + [1 / NOPE] * 4
    cst[:, K_I8:K_I8 + 8] = np.arange(8)
    cst[:, K_TILE:K_TILE + NT] = np.arange(NT) * P
    cst[:, K_P] = np.arange(P)
    cst[:, K_TRI:K_TRI + P] = np.triu(np.ones((P, P)), 1)
    cst[:, K_NH:] = -0.5
    dist = np.abs(np.arange(P)[:, None] - np.arange(1920)[None, :] + (SEQ - P))
    alibi = np.stack([dist * 2.0 ** (-8.0 * (h + 1) / DH) for h in range(DH)], axis=1).astype(np.float16)
    t = np.arange(SEQ)
    count = [np.minimum(t + w // 2 - 1, SEQ - 1) - np.maximum(t - w // 2, 0) + 1 for w in WINDOWS]
    inv_count = np.ascontiguousarray(np.broadcast_to(np.stack([(1.0 / c).astype(f) for c in count])[:, None], (4, 64, SEQ)))
    iota = np.ascontiguousarray(np.broadcast_to(np.arange(SEQ + CAP, dtype=f), (P, SEQ + CAP)))

    nc = bacc.Bacc("TRN2", target_bir_lowering=False, num_devices=1)
    arrays, args = {}, []
    for name, a in (("x", x), ("w_in", w_in), ("w_uq", mla_w_uq), ("w_ukv", mla_w_ukv), ("pool_w", pw),
                    ("w_out", w_out), ("w_router", wr), ("w_gate", expert_w_gate), ("w_up", expert_w_up),
                    ("w_down", expert_w_down), ("small", small.transpose(1, 0, 2)), ("gain_rows", gain_rows), ("consts", cst),
                    ("alibi", alibi), ("inv_count", inv_count), ("iota", iota)):
        a = np.ascontiguousarray(a)
        arrays[f"in_{name}"] = a
        args.append(nc.dram_tensor(f"in_{name}", a.shape, mybir.dt.from_np(a.dtype), kind="ExternalInput").ap())
    out = nc.dram_tensor("out_0", (1, SEQ, D), F32, kind="ExternalOutput").ap()
    program(nc, *args, out)
    r = run_bass_kernel_spmd(nc, [arrays], core_ids=[0])
    return r.results[0]["out_0"]
```
